# Optimizing a Trainium2 kernel written in Bass

```python
import math
import jax
import jax.numpy as jnp
from jax import lax
import numpy as np
import jax, jax.numpy as jnp

D_MODEL = 1024
BATCH = 1
SEQ = 256
DEPTH = 2

N_HEADS = 8
N_KV_HEADS = 2
HEAD_DIM = 64
Q_PER_KV = N_HEADS // N_KV_HEADS
ATTN_WIDTH = N_HEADS * HEAD_DIM
KV_WIDTH = N_KV_HEADS * HEAD_DIM
N_BRANCH = 3
CMP_LEN = 32
CMP_STRIDE = 16
CMP_HIDDEN = 128
SEL_LEN = 64
SEL_TOPK = 16
N_LOCAL_SEL = 2
WINDOW = 512
Q_BLOCK = 64
CONV_WIDTH = D_MODEL // 2
CONV_KERNEL = 31
MIX_WIDTH = ATTN_WIDTH + CONV_WIDTH
IN_WIDTH = ATTN_WIDTH + 6 * KV_WIDTH + N_HEADS * N_BRANCH + 2 * CONV_WIDTH
ROPE_THETA = 500000.0
ROPE_DIM = HEAD_DIM // 4
D_FF = 7 * D_MODEL // 2
N_EXPERTS = 8
TOP_K = 2
MOE_BLOCK = 128
EPS = 1e-6


def rms_norm(x, g):
    xf = x.astype(jnp.float32)
    y = xf * lax.rsqrt(jnp.mean(xf * xf, axis=-1, keepdims=True) + EPS)
    return (y * g.astype(jnp.float32)).astype(x.dtype)

def layer_norm(x, g, b):
    xf = x.astype(jnp.float32)
    xc = xf - jnp.mean(xf, axis=-1, keepdims=True)
    y = xc * lax.rsqrt(jnp.mean(xc * xc, axis=-1, keepdims=True) + EPS)
    return (y * g.astype(jnp.float32) + b.astype(jnp.float32)).astype(x.dtype)

def masked_softmax(s, mask):
    s = jnp.where(mask, s.astype(jnp.float32), -jnp.inf)
    m = jnp.max(s, axis=-1, keepdims=True)
    m = jnp.where(jnp.isfinite(m), m, 0.0)
    p = jnp.exp(s - m)
    return p / jnp.maximum(jnp.sum(p, axis=-1, keepdims=True), jnp.finfo(jnp.float32).tiny)

def rope_partial(x, pos):
    half = ROPE_DIM // 2
    inv_freq = ROPE_THETA ** (-2.0 * jnp.arange(half, dtype=jnp.float32) / ROPE_DIM)
    ang = pos.astype(jnp.float32)[..., None, None] * inv_freq
    cos, sin = jnp.cos(ang), jnp.sin(ang)
    xr = x[..., :ROPE_DIM].astype(jnp.float32)
    x1, x2 = xr[..., :half], xr[..., half:]
    rot = jnp.concatenate([x1 * cos - x2 * sin, x2 * cos + x1 * sin], axis=-1).astype(x.dtype)
    return jnp.concatenate([rot, x[..., ROPE_DIM:]], axis=-1)

def swiglu(x, wg, wu, wd):
    return (jax.nn.silu(x @ wg) * (x @ wu)) @ wd

def in_proj_split_points():
    sizes = [ATTN_WIDTH] + [KV_WIDTH] * 6 + [N_HEADS * N_BRANCH, 2 * CONV_WIDTH]
    return [int(v) for v in np.cumsum(sizes)[:-1]]

def n_cmp_blocks(s):
    return (s - CMP_LEN) // CMP_STRIDE + 1

def cmp_block_ends(s):
    return np.arange(n_cmp_blocks(s)) * CMP_STRIDE + CMP_LEN - 1

def selection_map(s):
    c0 = np.arange(n_cmp_blocks(s)) * CMP_STRIDE
    s0 = np.arange(s // SEL_LEN) * SEL_LEN
    ov = np.minimum(c0[:, None] + CMP_LEN, s0[None, :] + SEL_LEN) - np.maximum(c0[:, None], s0[None, :])
    return jnp.asarray(np.clip(ov, 0, None) / CMP_LEN, dtype=jnp.float32)

def compress_blocks(kv, pos_emb, w1, w2):
    b, s = kv.shape[0], kv.shape[1]
    n_cmp = n_cmp_blocks(s)
    idx = np.arange(n_cmp)[:, None] * CMP_STRIDE + np.arange(CMP_LEN)[None, :]
    blocks = kv[:, idx] + pos_emb[None, None, :, None, :]
    blocks = blocks.transpose(0, 1, 3, 2, 4).reshape(b, n_cmp, N_KV_HEADS, CMP_LEN * HEAD_DIM)
    hid = jax.nn.gelu(jnp.einsum('bnkf,fh->bnkh', blocks, w1))
    return jnp.einsum('bnkh,hd->bnkd', hid, w2)

def nsa_attention(q, k_cmp, v_cmp, k_slc, v_slc, k_win, v_win, gates):
    b, s = q.shape[0], q.shape[1]
    n_sel = s // SEL_LEN
    top_n = min(SEL_TOPK, n_sel)
    scale = HEAD_DIM ** -0.5
    q = q.reshape(b, s, N_KV_HEADS, Q_PER_KV, HEAD_DIM)
    gates = gates.reshape(b, s, N_KV_HEADS, Q_PER_KV, N_BRANCH)
    cmp_end = jnp.asarray(cmp_block_ends(s))
    sel_map = selection_map(s)
    k_blk = k_slc.reshape(b, n_sel, SEL_LEN, N_KV_HEADS, HEAD_DIM).transpose(0, 3, 1, 2, 4)
    v_blk = v_slc.reshape(b, n_sel, SEL_LEN, N_KV_HEADS, HEAD_DIM).transpose(0, 3, 1, 2, 4)
    pad = ((0, 0), (WINDOW, 0), (0, 0), (0, 0))
    k_wpad = jnp.pad(k_win, pad)
    v_wpad = jnp.pad(v_win, pad)
    b_ix = jnp.arange(b)[:, None, None, None]
    h_ix = jnp.arange(N_KV_HEADS)[None, None, :, None]
    blk_ids = jnp.arange(n_sel)

    def query_block(c):
        t0 = c * Q_BLOCK
        t = t0 + jnp.arange(Q_BLOCK)
        qc = lax.dynamic_slice_in_dim(q, t0, Q_BLOCK, axis=1)
        gc = lax.dynamic_slice_in_dim(gates, t0, Q_BLOCK, axis=1)
        s_c = jnp.einsum('bqkgd,bnkd->bqkgn', qc, k_cmp) * scale
        mask_c = (cmp_end[None, :] <= t[:, None])[None, :, None, None, :]
        p_c = masked_softmax(s_c, mask_c)
        o_c = jnp.einsum('bqkgn,bnkd->bqkgd', p_c.astype(v_cmp.dtype), v_cmp)
        imp = jnp.einsum('bqkgn,nj->bqkj', p_c, sel_map)
        cur = (t // SEL_LEN)[:, None]
        causal_blk = blk_ids[None, :] <= cur
        forced = (blk_ids[None, :] == 0) | (causal_blk & (blk_ids[None, :] > cur - N_LOCAL_SEL))
        score = jnp.where(forced[None, :, None, :], jnp.inf,
                          jnp.where(causal_blk[None, :, None, :], imp, -jnp.inf))
        _, sel_idx = lax.top_k(score, top_n)
        k_sel = k_blk[b_ix, h_ix, sel_idx].reshape(b, Q_BLOCK, N_KV_HEADS, top_n * SEL_LEN, HEAD_DIM)
        v_sel = v_blk[b_ix, h_ix, sel_idx].reshape(b, Q_BLOCK, N_KV_HEADS, top_n * SEL_LEN, HEAD_DIM)
        tok = (sel_idx[..., None] * SEL_LEN + jnp.arange(SEL_LEN)).reshape(
            b, Q_BLOCK, N_KV_HEADS, 1, top_n * SEL_LEN)
        mask_s = tok <= t[None, :, None, None, None]
        s_s = jnp.einsum('bqkgd,bqkmd->bqkgm', qc, k_sel) * scale
        p_s = masked_softmax(s_s, mask_s)
        o_s = jnp.einsum('bqkgm,bqkmd->bqkgd', p_s.astype(v_sel.dtype), v_sel)
        k_w = lax.dynamic_slice_in_dim(k_wpad, t0, WINDOW + Q_BLOCK, axis=1)
        v_w = lax.dynamic_slice_in_dim(v_wpad, t0, WINDOW + Q_BLOCK, axis=1)
        src = t0 - WINDOW + jnp.arange(WINDOW + Q_BLOCK)
        mask_w = ((src[None, :] >= 0) & (src[None, :] <= t[:, None])
                  & (src[None, :] > t[:, None] - WINDOW))[None, :, None, None, :]
        s_w = jnp.einsum('bqkgd,bwkd->bqkgw', qc, k_w) * scale
        p_w = masked_softmax(s_w, mask_w)
        o_w = jnp.einsum('bqkgw,bwkd->bqkgd', p_w.astype(v_w.dtype), v_w)
        return gc[..., 0:1] * o_c + gc[..., 1:2] * o_s + gc[..., 2:3] * o_w

    out = lax.map(query_block, jnp.arange(s // Q_BLOCK))
    return out.transpose(1, 0, 2, 3, 4, 5).reshape(b, s, ATTN_WIDTH)

def conformer_conv(u, conv_w, conv_b, ln_g, ln_b):
    a, g = jnp.split(u, 2, axis=-1)
    h = a * jax.nn.sigmoid(g)
    h = jnp.pad(h, ((0, 0), (CONV_KERNEL - 1, 0), (0, 0)))
    y = lax.conv_general_dilated(h, conv_w[:, None, :], window_strides=(1,), padding='VALID',
                                 dimension_numbers=('NWC', 'WIO', 'NWC'),
                                 feature_group_count=CONV_WIDTH)
    y = y + conv_b
    return jax.nn.silu(layer_norm(y, ln_g, ln_b))

def moe_swiglu(h, router, wg, wu, wd):
    b, s, d = h.shape
    n_tok = b * s
    xt = h.reshape(n_tok, d)
    logits = (xt @ router).astype(jnp.float32)
    top_logit, top_e = lax.top_k(logits, TOP_K)
    gate = jax.nn.softmax(top_logit, axis=-1)
    n_asg = n_tok * TOP_K
    e_flat = top_e.reshape(n_asg)
    tok_flat = jnp.broadcast_to(jnp.arange(n_tok)[:, None], (n_tok, TOP_K)).reshape(n_asg)
    g_flat = gate.reshape(n_asg)
    order = jnp.argsort(e_flat)
    e_s, tok_s, g_s = e_flat[order], tok_flat[order], g_flat[order]
    counts = jnp.bincount(e_flat, length=N_EXPERTS)
    padded = (counts + MOE_BLOCK - 1) // MOE_BLOCK * MOE_BLOCK
    start = jnp.cumsum(counts) - counts
    pend = jnp.cumsum(padded)
    pstart = pend - padded
    dest = pstart[e_s] + jnp.arange(n_asg) - start[e_s]
    n_blocks = -(-n_asg // MOE_BLOCK) + N_EXPERTS
    n_slots = n_blocks * MOE_BLOCK
    slot_tok = jnp.full((n_slots,), n_tok, jnp.int32).at[dest].set(tok_s.astype(jnp.int32))
    slot_gate = jnp.zeros((n_slots,), jnp.float32).at[dest].set(g_s)
    blk_e = jnp.clip(jnp.searchsorted(pend, jnp.arange(n_blocks) * MOE_BLOCK, side='right'),
                     0, N_EXPERTS - 1)
    x_pad = jnp.concatenate([xt, jnp.zeros((1, d), xt.dtype)], axis=0)
    xs = x_pad[slot_tok].reshape(n_blocks, MOE_BLOCK, d)

    def expert_block(args):
        xb, e = args
        return swiglu(xb, wg[e], wu[e], wd[e])

    ys = lax.map(expert_block, (xs, blk_e)).reshape(n_slots, d)
    ys = ys * slot_gate[:, None].astype(ys.dtype)
    out = jax.ops.segment_sum(ys, slot_tok, num_segments=n_tok + 1)[:n_tok]
    return out.reshape(b, s, d)

def first_inputs(seed: int = 0) -> dict:
    key = jax.random.key(seed)
    keys = list(jax.random.split(key, 32))

    def nrm(i, shape, scale):
        return scale * jax.random.normal(keys[i], shape, jnp.float32)

    n_dense = (DEPTH + 1) // 2
    n_moe = DEPTH // 2
    x = nrm(0, (BATCH, SEQ, D_MODEL), 1.0)
    offsets = jax.random.randint(keys[1], (BATCH, 1), 0, 2048, dtype=jnp.int32)
    positions = offsets + jnp.arange(SEQ, dtype=jnp.int32)[None, :]
    return {
        "x": x,
        "positions": positions,
        "attn_norm_g": 1.0 + nrm(2, (DEPTH, D_MODEL), 0.02),
        "ffn_norm_g": 1.0 + nrm(3, (DEPTH, D_MODEL), 0.02),
        "w_in": nrm(4, (DEPTH, D_MODEL, IN_WIDTH), D_MODEL ** -0.5),
        "w_out": nrm(5, (DEPTH, MIX_WIDTH, D_MODEL), MIX_WIDTH ** -0.5),
        "q_norm_g": 1.0 + nrm(6, (DEPTH, HEAD_DIM), 0.02),
        "k_norm_g": 1.0 + nrm(7, (DEPTH, N_BRANCH, HEAD_DIM), 0.02),
        "cmp_pos_k": nrm(8, (DEPTH, CMP_LEN, HEAD_DIM), 0.1),
        "cmp_w1_k": nrm(9, (DEPTH, CMP_LEN * HEAD_DIM, CMP_HIDDEN), (CMP_LEN * HEAD_DIM) ** -0.5),
        "cmp_w2_k": nrm(10, (DEPTH, CMP_HIDDEN, HEAD_DIM), CMP_HIDDEN ** -0.5),
        "cmp_pos_v": nrm(11, (DEPTH, CMP_LEN, HEAD_DIM), 0.1),
        "cmp_w1_v": nrm(12, (DEPTH, CMP_LEN * HEAD_DIM, CMP_HIDDEN), (CMP_LEN * HEAD_DIM) ** -0.5),
        "cmp_w2_v": nrm(13, (DEPTH, CMP_HIDDEN, HEAD_DIM), CMP_HIDDEN ** -0.5),
        "conv_w": nrm(14, (DEPTH, CONV_KERNEL, CONV_WIDTH), CONV_KERNEL ** -0.5),
        "conv_b": nrm(15, (DEPTH, CONV_WIDTH), 0.02),
        "conv_ln_g": 1.0 + nrm(16, (DEPTH, CONV_WIDTH), 0.02),
        "conv_ln_b": nrm(17, (DEPTH, CONV_WIDTH), 0.02),
        "ffn_w_gate": nrm(18, (n_dense, D_MODEL, D_FF), D_MODEL ** -0.5),
        "ffn_w_up": nrm(19, (n_dense, D_MODEL, D_FF), D_MODEL ** -0.5),
        "ffn_w_down": nrm(20, (n_dense, D_FF, D_MODEL), D_FF ** -0.5),
        "moe_router": nrm(21, (n_moe, D_MODEL, N_EXPERTS), D_MODEL ** -0.5),
        "moe_w_gate": nrm(22, (n_moe, N_EXPERTS, D_MODEL, D_FF), D_MODEL ** -0.5),
        "moe_w_up": nrm(23, (n_moe, N_EXPERTS, D_MODEL, D_FF), D_MODEL ** -0.5),
        "moe_w_down": nrm(24, (n_moe, N_EXPERTS, D_FF, D_MODEL), D_FF ** -0.5),
    }

def first_block(x, positions, attn_norm_g, ffn_norm_g, w_in, w_out, q_norm_g, k_norm_g,
              cmp_pos_k, cmp_w1_k, cmp_w2_k, cmp_pos_v, cmp_w1_v, cmp_w2_v,
              conv_w, conv_b, conv_ln_g, conv_ln_b,
              ffn_w_gate, ffn_w_up, ffn_w_down,
              moe_router, moe_w_gate, moe_w_up, moe_w_down):
    b, s, _ = x.shape
    pos_cmp = positions[:, cmp_block_ends(s)]
    split_points = in_proj_split_points()
    for layer in range(DEPTH):
        h = rms_norm(x, attn_norm_g[layer])
        proj = jnp.einsum('bsd,de->bse', h, w_in[layer])
        q, k_c, v_c, k_s, v_s, k_w, v_w, g_logit, u = jnp.split(proj, split_points, axis=-1)
        q = rope_partial(rms_norm(q.reshape(b, s, N_HEADS, HEAD_DIM), q_norm_g[layer]), positions)
        kv_shape = (b, s, N_KV_HEADS, HEAD_DIM)
        k_cmp = compress_blocks(k_c.reshape(kv_shape), cmp_pos_k[layer], cmp_w1_k[layer], cmp_w2_k[layer])
        k_cmp = rope_partial(rms_norm(k_cmp, k_norm_g[layer, 0]), pos_cmp)
        v_cmp = compress_blocks(v_c.reshape(kv_shape), cmp_pos_v[layer], cmp_w1_v[layer], cmp_w2_v[layer])
        k_slc = rope_partial(rms_norm(k_s.reshape(kv_shape), k_norm_g[layer, 1]), positions)
        k_win = rope_partial(rms_norm(k_w.reshape(kv_shape), k_norm_g[layer, 2]), positions)
        gates = jax.nn.sigmoid(g_logit.astype(jnp.float32)).astype(x.dtype).reshape(b, s, N_HEADS, N_BRANCH)
        attn_out = nsa_attention(q, k_cmp, v_cmp, k_slc, v_s.reshape(kv_shape),
                                 k_win, v_w.reshape(kv_shape), gates)
        conv_out = conformer_conv(u, conv_w[layer], conv_b[layer], conv_ln_g[layer], conv_ln_b[layer])
        mixed = jnp.concatenate([attn_out, conv_out], axis=-1)
        x = x + jnp.einsum('bsm,md->bsd', mixed, w_out[layer])
        h = rms_norm(x, ffn_norm_g[layer])
        if layer % 2 == 0:
            i = layer // 2
            x = x + swiglu(h, ffn_w_gate[i], ffn_w_up[i], ffn_w_down[i])
        else:
            i = layer // 2
            x = x + moe_swiglu(h, moe_router[i], moe_w_gate[i], moe_w_up[i], moe_w_down[i])
    return x


GRID_W = 64
A_Q_HEADS = 8
A_KV_HEADS = 2
A_GROUP = A_Q_HEADS // A_KV_HEADS
B_HEADS = 4
B_V_DIM = 2 * HEAD_DIM
A_WIDTH = A_Q_HEADS * HEAD_DIM
B_WIDTH = B_HEADS * B_V_DIM
A_Q_COLS = A_Q_HEADS * HEAD_DIM
A_KV_COLS = A_KV_HEADS * HEAD_DIM
B_QK_COLS = 2 * B_HEADS * HEAD_DIM
B_V_COLS = B_HEADS * B_V_DIM
IN_COLS = A_Q_COLS + 2 * A_KV_COLS + 2 * B_QK_COLS + B_V_COLS
N_BRANCH_2 = 2
D_FF_2 = 2816
Q_BLOCK_2 = 128
ROPE_THETA_2 = 10000.0
ROPE_AXIS_DIM = HEAD_DIM // 2
N_ADA = 9


def rms_norm_2(x, g):
    xf = x.astype(jnp.float32)
    y = xf * lax.rsqrt(jnp.mean(xf * xf, axis=-1, keepdims=True) + EPS)
    return (y * g.astype(jnp.float32)).astype(x.dtype)

def modulate(x, shift, scale):
    return x * (1 + scale[:, None, :]) + shift[:, None, :]

def swiglu_2(x, w_gate, w_up, w_down):
    return (jax.nn.silu(x @ w_gate) * (x @ w_up)) @ w_down

def axial_angles(seq):
    rows = seq // GRID_W
    row = jnp.broadcast_to(jnp.arange(rows)[:, None], (rows, GRID_W)).reshape(seq) - rows // 2
    col = jnp.broadcast_to(jnp.arange(GRID_W)[None, :], (rows, GRID_W)).reshape(seq) - GRID_W // 2
    inv = 1.0 / (ROPE_THETA_2 ** (jnp.arange(0, ROPE_AXIS_DIM, 2, dtype=jnp.float32) / ROPE_AXIS_DIM))
    ang_r = row.astype(jnp.float32)[:, None] * inv
    ang_c = col.astype(jnp.float32)[:, None] * inv
    return ang_r, ang_c

def rotate_section(x, ang):
    cos = jnp.cos(ang)[:, None, :]
    sin = jnp.sin(ang)[:, None, :]
    x1, x2 = jnp.split(x, 2, axis=-1)
    return jnp.concatenate([x1 * cos - x2 * sin, x2 * cos + x1 * sin], axis=-1)

def axial_rope(x, ang_r, ang_c):
    xf = x.astype(jnp.float32)
    xr, xc = jnp.split(xf, 2, axis=-1)
    return jnp.concatenate([rotate_section(xr, ang_r), rotate_section(xc, ang_c)], axis=-1).astype(x.dtype)

def gqa_attention(q, k, v):
    b, s = q.shape[0], q.shape[1]
    nblk = s // Q_BLOCK_2
    qb = q.reshape(b, nblk, Q_BLOCK_2, A_KV_HEADS, A_GROUP, HEAD_DIM).transpose(1, 0, 2, 3, 4, 5)
    scale = HEAD_DIM ** -0.5

    def block(qi):
        sc = jnp.einsum('bqkgd,bskd->bkgqs', qi, k, preferred_element_type=jnp.float32) * scale
        p = jax.nn.softmax(sc, axis=-1).astype(v.dtype)
        return jnp.einsum('bkgqs,bskd->bqkgd', p, v)

    o = lax.map(block, qb)
    return o.transpose(1, 0, 2, 3, 4, 5).reshape(b, s, A_WIDTH)

def diff_attention(q, k, v, lam, slopes):
    b, s = q.shape[0], q.shape[1]
    nblk = s // Q_BLOCK_2
    qb = q.reshape(b, nblk, Q_BLOCK_2, 2, B_HEADS, HEAD_DIM).transpose(1, 0, 2, 3, 4, 5)
    scale = HEAD_DIM ** -0.5
    kpos = jnp.arange(s, dtype=jnp.float32)

    def block(args):
        qi, bi = args
        qpos = (bi * Q_BLOCK_2 + jnp.arange(Q_BLOCK_2)).astype(jnp.float32)
        dist = jnp.abs(qpos[:, None] - kpos[None, :])
        bias = -slopes[:, None, None] * dist[None]
        sc = jnp.einsum('bqmhd,bsmhd->bmhqs', qi, k, preferred_element_type=jnp.float32) * scale
        p = jax.nn.softmax(sc + bias[None, None], axis=-1)
        w = (p[:, 0] - lam * p[:, 1]).astype(v.dtype)
        return jnp.einsum('bhqs,bshe->bqhe', w, v)

    o = lax.map(block, (qb, jnp.arange(nblk)))
    return o.transpose(1, 0, 2, 3, 4).reshape(b, s, B_HEADS, B_V_DIM)

def token_mixing(n, ang_r, ang_c, lam_init, w_in, qk_g, lam_p, subln_g, w_ba, w_bb, w_gate, b_gate, w_o):
    b, s, _ = n.shape
    proj = n @ w_in
    c1 = A_Q_COLS
    c2 = c1 + A_KV_COLS
    c3 = c2 + A_KV_COLS
    c4 = c3 + B_QK_COLS
    c5 = c4 + B_QK_COLS
    qa, ka, va, qd, kd, vd = jnp.split(proj, [c1, c2, c3, c4, c5], axis=-1)

    qa = axial_rope(rms_norm_2(qa.reshape(b, s, A_Q_HEADS, HEAD_DIM), qk_g[0]), ang_r, ang_c)
    ka = axial_rope(rms_norm_2(ka.reshape(b, s, A_KV_HEADS, HEAD_DIM), qk_g[1]), ang_r, ang_c)
    va = va.reshape(b, s, A_KV_HEADS, HEAD_DIM)
    qa = qa.reshape(b, s, A_KV_HEADS, A_GROUP, HEAD_DIM)
    ya = gqa_attention(qa, ka, va) @ w_ba

    lp = lam_p.astype(jnp.float32)
    lam = jnp.exp(jnp.sum(lp[0] * lp[1])) - jnp.exp(jnp.sum(lp[2] * lp[3])) + lam_init
    slopes = 2.0 ** (-8.0 * jnp.arange(1, B_HEADS + 1, dtype=jnp.float32) / B_HEADS)
    qd = qd.reshape(b, s, 2, B_HEADS, HEAD_DIM)
    kd = kd.reshape(b, s, 2, B_HEADS, HEAD_DIM)
    vd = vd.reshape(b, s, B_HEADS, B_V_DIM)
    od = diff_attention(qd, kd, vd, lam, slopes)
    od = rms_norm_2(od, subln_g) * (1.0 - lam_init)
    yb = od.reshape(b, s, B_WIDTH) @ w_bb

    g = jax.nn.sigmoid(n @ w_gate + b_gate)
    ga, gb = jnp.split(g, N_BRANCH_2, axis=-1)
    return (ga * ya + gb * yb) @ w_o

def second_inputs(seed: int = 0) -> dict:
    key = jax.random.key(seed)
    ks = jax.random.split(key, 24)
    D, L, F = D_MODEL, DEPTH, D_FF_2

    def nrm(k, shape, scale):
        return jax.random.normal(k, shape, jnp.float32) * scale

    return {
        'x': nrm(ks[0], (BATCH, SEQ, D), 1.0),
        'c': nrm(ks[1], (BATCH, D), 1.0),
        'ada_w': nrm(ks[2], (L, D, N_ADA * D), 0.5 * D ** -0.5),
        'ada_b': nrm(ks[3], (L, N_ADA * D), 0.01),
        'norm_g': 1.0 + nrm(ks[4], (L, 3, D), 0.02),
        'ffn_wg': nrm(ks[5], (L, 2, D, F), D ** -0.5),
        'ffn_wu': nrm(ks[6], (L, 2, D, F), D ** -0.5),
        'ffn_wd': nrm(ks[7], (L, 2, F, D), F ** -0.5),
        'w_in': nrm(ks[8], (L, D, IN_COLS), D ** -0.5),
        'qk_g': 1.0 + nrm(ks[9], (L, 2, HEAD_DIM), 0.02),
        'lam_p': nrm(ks[10], (L, 4, HEAD_DIM), 0.1),
        'subln_g': 1.0 + nrm(ks[11], (L, B_V_DIM), 0.02),
        'w_ba': nrm(ks[12], (L, A_WIDTH, D), A_WIDTH ** -0.5),
        'w_bb': nrm(ks[13], (L, B_WIDTH, D), B_WIDTH ** -0.5),
        'w_gate': nrm(ks[14], (L, D, N_BRANCH_2 * D), D ** -0.5),
        'b_gate': nrm(ks[15], (L, N_BRANCH_2 * D), 0.01),
        'w_o': nrm(ks[16], (L, D, D), D ** -0.5),
        'final_g': 1.0 + nrm(ks[17], (D,), 0.02),
    }

def second_block(x, c, ada_w, ada_b, norm_g, ffn_wg, ffn_wu, ffn_wd, w_in, qk_g, lam_p, subln_g, w_ba, w_bb, w_gate, b_gate, w_o, final_g):
    s = x.shape[1]
    ang_r, ang_c = axial_angles(s)
    c_act = jax.nn.silu(c)
    h = x
    for l in range(DEPTH):
        mod = c_act @ ada_w[l] + ada_b[l]
        sh1, sc1, g1, sh2, sc2, g2, sh3, sc3, g3 = jnp.split(mod, N_ADA, axis=-1)
        lam_init = 0.8 - 0.6 * float(np.exp(-0.3 * l))

        n1 = modulate(rms_norm_2(h, norm_g[l, 0]), sh1, sc1)
        h = h + 0.5 * g1[:, None, :] * swiglu_2(n1, ffn_wg[l, 0], ffn_wu[l, 0], ffn_wd[l, 0])

        n2 = modulate(rms_norm_2(h, norm_g[l, 1]), sh2, sc2)
        y = token_mixing(n2, ang_r, ang_c, lam_init, w_in[l], qk_g[l], lam_p[l], subln_g[l],
                         w_ba[l], w_bb[l], w_gate[l], b_gate[l], w_o[l])
        h = h + g2[:, None, :] * y

        n3 = modulate(rms_norm_2(h, norm_g[l, 2]), sh3, sc3)
        h = h + 0.5 * g3[:, None, :] * swiglu_2(n3, ffn_wg[l, 1], ffn_wu[l, 1], ffn_wd[l, 1])
    return rms_norm_2(h, final_g)


def setup_inputs(seed=0):
    out = dict(first_inputs(seed))
    for name, value in second_inputs(seed + 1).items():
        if name != "x":
            out[name + "_2"] = value
    return out


def reference(
    x, positions, attn_norm_g, ffn_norm_g, w_in, w_out, q_norm_g, k_norm_g, cmp_pos_k, cmp_w1_k,
    cmp_w2_k, cmp_pos_v, cmp_w1_v, cmp_w2_v, conv_w, conv_b, conv_ln_g, conv_ln_b, ffn_w_gate,
    ffn_w_up, ffn_w_down, moe_router, moe_w_gate, moe_w_up, moe_w_down, c_2, ada_w_2, ada_b_2,
    norm_g_2, ffn_wg_2, ffn_wu_2, ffn_wd_2, w_in_2, qk_g_2, lam_p_2, subln_g_2, w_ba_2, w_bb_2,
    w_gate_2, b_gate_2, w_o_2, final_g_2,
):
    x = first_block(
        x, positions, attn_norm_g, ffn_norm_g, w_in, w_out, q_norm_g, k_norm_g, cmp_pos_k,
        cmp_w1_k, cmp_w2_k, cmp_pos_v, cmp_w1_v, cmp_w2_v, conv_w, conv_b, conv_ln_g, conv_ln_b,
        ffn_w_gate, ffn_w_up, ffn_w_down, moe_router, moe_w_gate, moe_w_up, moe_w_down,
    )
    return second_block(
        x, c_2, ada_w_2, ada_b_2, norm_g_2, ffn_wg_2, ffn_wu_2, ffn_wd_2, w_in_2, qk_g_2,
        lam_p_2, subln_g_2, w_ba_2, w_bb_2, w_gate_2, b_gate_2, w_o_2, final_g_2,
    )


_drawn_inputs = setup_inputs


def setup_inputs(seed=0):
    import zlib

    import numpy as np

    out = dict(_drawn_inputs(seed))
    spreads = {}
    factors = {'q_norm_g': 5.51,
     'k_norm_g': 4.051,
     'cmp_pos_k': 7.368,
     'conv_ln_b': 3.064,
     'ada_b_2': 6.824,
     'norm_g_2': 8.0,
     'qk_g_2': 8.0,
     'lam_p_2': 4.784,
     'subln_g_2': 41.829,
     'b_gate_2': 52.912,
     'final_g_2': 8.274}
    for name, (base, spread) in spreads.items():
        noise = np.random.default_rng([zlib.crc32(name.encode()), seed]).standard_normal(out[name].shape)
        drawn = base * np.exp(spread * noise) if base else spread * noise
        out[name] = jnp.asarray(drawn.astype(out[name].dtype))
    for name, factor in factors.items():
        out[name] = (out[name] * factor).astype(out[name].dtype)
    return out
```

```python
from contextlib import ExitStack

import numpy as np
import concourse.bass as bass
from concourse import mybir

ALU = mybir.AluOpType
ACT = mybir.ActivationFunctionType
F32 = mybir.dt.float32
I32 = mybir.dt.int32
U32 = mybir.dt.uint32
AX = mybir.AxisListType.X
MUL, ADD, SUB, MAX, MIN = ALU.mult, ALU.add, ALU.subtract, ALU.max, ALU.min

P = 128
D = 1024
S = 256
NS = 5
EPS = 1e-6
NEG = -1e30
NE = 8
F1 = 3584
F2 = 2816
NCMP = 15
TWO_PI = 6.283185307179586
MAGIC = 12582912.0

CI, CO, CC, CM, CV, CF, CD, CA, CT, CR = np.cumsum([0, 128, 128, 128, 30, 2, 8, 512, 128, 128]).tolist()
NCONST = CR + 256
CAP = 128


def constants():
    c = np.zeros((P, NCONST), np.float32)
    p = np.arange(P)
    c[:, CI:CI + 128] = np.eye(P)
    c[:, CO:CO + 128] = 1.0
    c[:, CC:CC + 128] = np.where(p[None, :] <= p[:, None], 0.0, NEG)
    ends = np.arange(NCMP) * 16 + 31
    for b in range(2):
        t = b * P + p
        ok = ends[None, :] <= t[:, None]
        c[:, CM + b * 15:CM + b * 15 + 15] = np.where(ok, 0.0, NEG)
        c[:, CV + b] = ok.any(1)
        c[:, CD + b * 256:CD + b * 256 + 256] = np.abs(t[:, None] - np.arange(256)[None, :])
        inv = 1.0 / (np.float32(10000.0) ** (np.arange(0, 32, 2, dtype=np.float32) / 32))
        row = (t // 64 - 2).astype(np.float32)
        col = (t % 64 - 32).astype(np.float32)
        ang = np.stack([row[:, None] * inv, col[:, None] * inv], 1)
        c[:, CA + b * 64:CA + b * 64 + 32] = np.cos(ang).reshape(P, 32)
        c[:, CA + b * 64 + 32:CA + b * 64 + 64] = np.sin(ang).reshape(P, 32)
    c[:, CF:CF + 8] = (500000.0 ** (-2.0 * np.arange(8) / 16)).astype(np.float32)[None]
    c[:, CT:CT + 128] = p[:, None] < p[None, :]
    c[:, CR:CR + 128] = np.where(p < CAP, p, -1)[None, :]
    c[:, CR + 128:CR + 256] = p[None, :] + CAP
    return c


class Queue:

    def __init__(self, sem):
        self.sem, self.n, self.q, self.seen = sem, 0, [], {}

    def wait(self, *toks):
        for t in toks:
            if t is not None and self.seen.get(t[0].name, 0) < t[1]:
                self.seen[t[0].name] = t[1]
                self.q.append(lambda e, t=t: e.wait_ge(t[0], t[1]))

    def do(self, f, *w):
        self.wait(*w)
        self.q.append(f)

    def inc(self, f, *w):
        self.wait(*w)
        self.n += 1
        self.q.append(lambda e: f(e).then_inc(self.sem, 1))
        return (self.sem, self.n)

    def run(self, e):
        for f in self.q:
            f(e)


class PE(Queue):
    def mm(self, out, lhsT, rhs, start, stop, *w, last=False):
        def f(e):
            return e.matmul(out, lhsT, rhs, start=start, stop=stop)
        if last:
            return self.inc(f, *w)
        self.do(f, *w)

    def tr(self, out, in_, ident, *w, last=False):
        def f(e):
            return e.transpose(out, in_, ident)
        if last:
            return self.inc(f, *w)
        self.do(f, *w)


class DVE(Queue):
    def tt(self, out, a, b, op, *w):
        return self.inc(lambda e: e.tensor_tensor(out, a, b, op), *w)

    def ts(self, out, a, s1, s2, op0, op1, *w):
        if s2 is None:
            return self.inc(lambda e: e.tensor_scalar(out, a, s1, None, op0), *w)
        return self.inc(lambda e: e.tensor_scalar(out, a, s1, s2, op0, op1), *w)

    def stt(self, out, a, s, b, op0, op1, *w):
        return self.inc(lambda e: e.scalar_tensor_tensor(out=out, in0=a, scalar=s, in1=b, op0=op0, op1=op1), *w)

    def rcp(self, out, a, *w):
        return self.inc(lambda e: e.reciprocal(out, a), *w)

    def rsqrt(self, y, x, a, *w):
        t = self.ts(y.bitcast(I32), x.bitcast(I32), -0.5, 1597463007.0, MUL, ADD, *w)
        t = self.ts(x, x, -0.5, None, MUL, None, t)
        for _ in range(3):
            t = self.tt(a, y, y, MUL, t)
            t = self.tt(a, a, x, MUL, t)
            t = self.stt(y, a, 1.5, y, ADD, MUL, t)
        return t

    def red(self, out, a, op, *w, neg=False):
        return self.inc(lambda e: e.tensor_reduce(out, a, AX, op, negate=neg), *w)

    def cp(self, out, a, *w):
        return self.inc(lambda e: e.tensor_copy(out, a), *w)

    def ms(self, out, v, *w):
        return self.inc(lambda e: e.memset(out, v), *w)


class SCA(Queue):
    def act(self, out, a, func, *w, bias=0.0, scale=1.0, acc=None):
        if acc is None:
            return self.inc(lambda e: e.activation(out, a, func, bias=bias, scale=scale), *w)
        return self.inc(lambda e: e.activation(out, a, func, bias=bias, scale=scale, accum_out=acc), *w)

    def cp(self, out, a, *w):
        return self.inc(lambda e: e.activation(out, a, ACT.Copy), *w)


def bc(ap, shape, at):
    for i in at:
        ap = ap.unsqueeze(i)
    return ap.to_broadcast(shape)


def build(nc, A, out):
    with ExitStack() as ctx:
        def sb(name, shape, dt=F32):
            return ctx.enter_context(nc.sbuf_tensor(name, shape, dt))

        def sem(name):
            return ctx.enter_context(nc.semaphore(name))

        pe, dve, sca, pool, sp = PE(sem("s_pe")), DVE(sem("s_dve")), SCA(sem("s_act")), DVE(sem("s_pool")), Queue(sem("s_sp"))
        PS = ctx.enter_context(nc.psum_tensor("PS", [P, 8, 512], F32))
        free = [None] * 8

        ring = sb("ring", [P, NS, 4096])
        s_ring = [sem(f"s_ring{i}") for i in range(NS)]
        C = sb("C", [P, NCONST])
        X = sb("X", [P, 2, D])
        XT = sb("XT", [P, 8, S])
        R = sb("R", [P, 4608 + 4096])
        PR = R[:, 0:4608]
        HT = R[:, 0:7168].rearrange("p (c n) -> p c n", c=28)
        PB = R[:, 4608:4608 + 2048].rearrange("p (g n) -> p g n", g=2)
        PTB = R[:, 4608 + 2048:4608 + 4096].rearrange("p (g n) -> p g n", g=2)
        TMP = R[:, 4608:4608 + 4096]
        XS = R[:, 4608:4608 + 2048].rearrange("p (b n) -> p b n", b=2)
        QT = sb("QT", [P, 8, S])
        EH = QT[:, :, :].rearrange("p a n -> p (a n)").rearrange("p (k i n) -> p k i n", k=2, i=2)
        KZ = sb("KZ", [P, 3072])
        MT = sb("MT", [P, 8, S])
        OA = sb("OA", [P, 2, 512])
        M2 = sb("M2", [P, 3700])
        GB = sb("GB", [P, D])
        ACC = sb("ACC", [P, 2, 512])
        VR = MT[:, 0:2, :].rearrange("p a (b n) -> p (a b) n", n=P)[:, 0:3, :]
        ADB = MT[0:72, 2, 0:P]
        VC = sb("VC", [P, 3, P])
        CWR = OA[0:31, :, :]
        CW = sb("CW", [P, 8, 31])
        W2 = sb("W2", [P, 4, 64])
        RT = sb("RT", [P, 8, 8])
        QKG = sb("QKG", [P, 2, 4, 64])
        QG2 = sb("QG2", [P, 2, 2, 64])
        LP = sb("LP", [P, 2, 256])
        SG = sb("SG", [P, 2, P])
        CACT = sb("CACT", [P, 2, 8])
        MODC = sb("MODC", [P, 2, 72])
        POSI = sb("POSI", [P, 3], I32)
        POSF = sb("POSF", [P, 3])
        CS = sb("CS", [P, 2, 3, 8])
        AN = sb("AN", [P, 4, 24])
        SM = sb("SM", [P, 512])
        MOSTI = sb("MOSTI", [P, 1], I32)

        ident = C[:, CI:CI + 128]
        ones = C[:, CO:CO + 128]

        cnt = [0] * NS
        rel = [None] * NS
        turn = [0]

        def slab(*parts):
            i = turn[0] % NS
            turn[0] += 1
            sp.wait(rel[i])
            views = []
            for src, at, c, w in parts:
                dst = ring[:, i, at:at + c * w].rearrange("p (c n) -> p c n", c=c)
                cnt[i] += 16
                sp.do(lambda e, dst=dst, src=src: e.dma_start(dst, src).then_inc(s_ring[i], 16))
                views.append(dst)
            return views, (s_ring[i], cnt[i]), i

        s_c, s_x, s_s = sem("s_c"), sem("s_x"), sem("s_s")
        sca.do(lambda e: e.dma_start(X[:, :, :], A["x"][0].rearrange("(b p) n -> p b n", p=P)).then_inc(s_x, 16))
        sca.do(lambda e: e.dma_start(C[:, :], A["cst"]).then_inc(s_c, 16))
        tc, tx = (s_c, 16), (s_x, 16)
        t0 = pool.ms(VR[:, :, :], 0.0)
        t1 = pool.ms(POSI[:, :], 0)
        ns = [0]

        def small(dst, src, odd=False):
            ns[0] += 16
            sca.do(lambda e: e.dma_start(dst, src, allow_slow_non_contiguous=odd).then_inc(s_s, 16), t0, t1)

        def rows(name):
            a = A[name]
            if len(a.shape) == 1:
                return a.rearrange("(r n) -> r n", n=P)
            if len(a.shape) == 2:
                return a.rearrange("l (r n) -> (l r) n", n=P)
            return a.rearrange("l k (r n) -> (l k r) n", n=P)

        VAT = {}
        for tile, names in enumerate((("attn_norm_g", "ffn_norm_g", "norm_g_2", "b_gate_2"),
                                      ("conv_b", "conv_ln_g", "conv_ln_b"), ())):
            r = 0
            for nm in names:
                a = rows(nm)
                n = a.shape[0]
                small(VR[r:r + n, tile, :], a)
                VAT[nm] = (tile, r)
                r += n
        for l in range(2):
            for j, nm in enumerate(("cmp_pos_k", "cmp_pos_v")):
                r = 24 + 32 * l + 16 * j
                small(VR[r:r + 16, 1, :], A[nm][l].rearrange("(r t) d -> r (t d)", t=2))
                VAT[nm, l] = (1, r)
        small(VR[0:72, 2, :], A["ada_b_2"][0].rearrange("(r n) -> r n", n=P))
        small(ADB, A["ada_b_2"][1].rearrange("(r n) -> r n", n=P))
        small(CWR[:, :, :], A["conv_w"].rearrange("l k n -> k l n"))
        for l in range(2):
            for j, nm in enumerate(("cmp_w2_k", "cmp_w2_v")):
                small(W2[:, 2 * l + j, :], A[nm][l])
        small(RT[:, :, :], A["moe_router"][0].rearrange("(c p) e -> p c e", p=P))
        small(QKG[:, :, 0, :], A["q_norm_g"].partition_broadcast(P))
        small(QKG[:, :, 1:4, :], A["k_norm_g"].partition_broadcast(P))
        small(QG2[:, :, :, :], A["qk_g_2"].partition_broadcast(P))
        small(LP[:, :, :], A["lam_p_2"].rearrange("l a d -> l (a d)").partition_broadcast(P))
        small(SG[:, :, :], A["subln_g_2"].partition_broadcast(P))
        small(CACT[:, 0, :], A["c_2"][0].rearrange("(p c) -> p c", c=8))
        for b in range(2):
            small(POSI[:, b:b + 1], A["positions"][0, b * P:b * P + P].rearrange("(p a) -> p a", a=1))
        small(POSI[0:NCMP, 2:3], A["positions"][0, 16:256].rearrange("(n a) -> n a", a=16)[:, 15:16], odd=True)
        tsm = (s_s, ns[0])

        pe.wait(tc, tsm)
        for i in range(3):
            t = pe.tr(PS[:, i, 0:P], VR[:, i, :], ident, last=True)
            free[i] = dve.cp(VC[:, i, :], PS[:, i, 0:P], t)
        t = pe.tr(PS[:, 3, 0:72], ADB, ident[0:72, 0:72], last=True)
        ADC = sb("ADC", [P, 72])
        free[3] = dve.cp(ADC[:, :], PS[:, 3, 0:72], t)
        for j in range(8):
            t = pe.tr(PS[:, 4, 32 * j:32 * j + 31], CWR[:, j // 4, (j % 4) * P:(j % 4) * P + P], ident[0:31, 0:31],
                      last=(j == 7))
        tvc = free[4] = dve.cp(CW[:, :, :], PS[:, 4, 0:256].rearrange("p (j k) -> p j k", k=32)[:, :, 0:31], t)

        def vcol(nm, l, c, per=8):
            tile, r = VAT[nm]
            return VC[:, tile, r + l * per + c:r + l * per + c + 1]

        t = dve.cp(POSF[:, :], POSI[:, :], tsm)
        an = AN[:, 0, :].rearrange("p (s j) -> p s j", j=8)
        t = dve.tt(an, bc(POSF[:, :], [P, 3, 8], (2,)), bc(C[:, CF:CF + 8], [P, 3, 8], (1,)), MUL, t, tc)
        trope = []
        for j, shift in ((0, 0.25), (1, 0.0)):
            k, r = AN[:, 1, :], AN[:, 2 + j, :]
            t = dve.ts(k, AN[:, 0, :], 1.0 / TWO_PI, shift, MUL, ADD, t)
            t = dve.ts(k, k, MAGIC, None, ADD, None, t)
            t = dve.ts(k, k, MAGIC, None, SUB, None, t)
            c1 = 6.28125
            c2 = float(np.float32(TWO_PI - c1).view(np.uint32) & np.uint32(0xFFFFF000))
            c2 = float(np.uint32(int(c2)).view(np.float32))
            c3 = float(np.float32(TWO_PI - c1 - c2))
            t = dve.stt(r, k, -c1, AN[:, 0, :], MUL, ADD, t)
            t = dve.stt(r, k, -c2, r, MUL, ADD, t)
            t = dve.stt(r, k, -c3, r, MUL, ADD, t)
            t = dve.ts(r, r, TWO_PI * shift, 3.1415925, ADD, MIN, t)
            t = dve.ts(r, r, -3.1415925, None, MAX, None, t)
            trope.append(sca.act(CS[:, j, :, :].rearrange("p s j -> p (s j)"), r, ACT.Sin, t))
        trope = trope[1]

        t = sca.act(CACT[:, 1, :], CACT[:, 0, :], ACT.Sigmoid, tsm)
        tcact = dve.tt(CACT[:, 1, :], CACT[:, 0, :], CACT[:, 1, :], MUL, t)

        ada_tok = [None, None]
        ada_free = [None, None]

        def ada_steps():
            for l in range(2):
                for s in range(18):
                    (w,), tw, slot = slab((A["ada_w_2"][l][:, s * 512:s * 512 + 512].rearrange("(p c) n -> p c n", c=8),
                                           0, 8, 512))
                    a = ACC[:, s % 2, :]
                    t = dve.ts(a, w[:, 0, :], CACT[:, 1, 0:1], None, MUL, None, tw, tcact, ada_free[s % 2])
                    for c in range(1, 8):
                        t = dve.stt(a, w[:, c, :], CACT[:, 1, c:c + 1], a, MUL, ADD, t)
                    rel[slot] = t
                    yield
                    pe.wait(t, free[7])
                    for c in range(4):
                        t = pe.mm(PS[:, 7, c:c + 1], a[:, c * P:c * P + P], ones[:, 0:1], True, True, last=(c == 3))
                    ada_free[s % 2] = t
                    ab = VC[:, 2, 4 * s:4 * s + 4] if l == 0 else ADC[:, 4 * s:4 * s + 4]
                    free[7] = ada_tok[l] = dve.tt(MODC[:, l, 4 * s:4 * s + 4], PS[:, 7, 0:4], ab, ADD, t, tvc)
                    yield

        steps = ada_steps()

        def ada(n):
            for _ in range(2 * n):
                next(steps, None)

        next(steps)

        xtok = [tx, tx]

        def norm_turn(gain, shift, *w):
            ts = []
            for b in range(2):
                ts.append(sca.act(XS[:, b, :], X[:, b, :], ACT.Square, *xtok, acc=SM[:, b:b + 1]))
            t = dve.ts(SM[:, 2:4], SM[:, 0:2], 1.0 / D, EPS, MUL, ADD, *ts)
            t = dve.rsqrt(SM[:, 4:6], SM[:, 2:4], SM[:, 6:8], t)
            a = dve.ts(XS[:, 0, :], X[:, 0, :], SM[:, 4:5], None, MUL, None, t)
            b_ = sca.act(XS[:, 1, :], X[:, 1, :], ACT.Copy, t, scale=SM[:, 5:6])
            toks = [None] * 8
            pe.wait(a, b_, tc)
            for j in range(4):
                pe.wait(free[j])
                for cc in range(2):
                    c = 2 * j + cc
                    for b in range(2):
                        t = pe.tr(PS[:, j, cc * 256 + b * P:cc * 256 + b * P + P], XS[:, b, c * P:c * P + P], ident,
                                  last=(cc == 1 and b == 1))
                for cc in range(2):
                    c = 2 * j + cc
                    src = PS[:, j, cc * 256:cc * 256 + 256]
                    if j % 2:
                        k = dve.ts(XT[:, c, :], src, gain(c), shift(c) if shift else None, MUL, ADD, t, tvc, *w)
                    elif shift:
                        k = sca.act(XT[:, c, :], src, ACT.Identity, t, tvc, *w, scale=gain(c), bias=shift(c))
                    else:
                        k = sca.act(XT[:, c, :], src, ACT.Copy, t, tvc, *w, scale=gain(c))
                    toks[c] = free[j] = k
            return toks

        def swiglu(xt, F, wg, wu, wd, finish):
            tiles = [(f, min(512, F - f)) for f in range(0, F, 512)]
            units = [(s, b) for s in range(len(tiles)) for b in range(2)]
            ht = {}
            hv = {}
            efree = [None, None]
            hfree = [None, None]
            slabs = {}

            def turn_h(i):
                s, b = units[i]
                n = tiles[s][1] // P
                B = 4 + i % 2
                h = EH[:, 1, i % 2, 0:n * P].rearrange("p (m c) -> p c m", c=n)
                pe.wait(free[B], hv[i])
                for c in range(n):
                    t = pe.tr(PS[:, B, c * P:c * P + P], h[:, c, :], ident, last=(c == n - 1))
                hfree[i % 2] = t
                ht[s, b] = free[B] = sca.cp(HT[:, 4 * s:4 * s + n, b * P:b * P + P],
                                            PS[:, B, 0:n * P].rearrange("p (c n) -> p c n", c=n), t)

            for i, (s, b) in enumerate(units):
                f, w = tiles[s]
                if b == 0:
                    slabs[s] = [slab((a[:, f:f + w].rearrange("(c p) n -> p c n", p=P), 0, 8, w)) for a in (wg, wu)]
                g, u = PS[:, 2 * (i % 2), 0:w], PS[:, 2 * (i % 2) + 1, 0:w]
                tk = []
                for o, bank, ((wt,), tw, slot) in ((g, 2 * (i % 2), slabs[s][0]), (u, 2 * (i % 2) + 1, slabs[s][1])):
                    pe.wait(free[bank], tw)
                    for c in range(8):
                        t = pe.mm(o, XT[:, c, b * P:b * P + P], wt[:, c, :], c == 0, c == 7, xt[c], last=(c == 7))
                    tk.append(t)
                    if b == 1:
                        rel[slot] = t
                e, h = EH[:, 0, i % 2, 0:w], EH[:, 1, i % 2, 0:w]
                t = sca.act(e, g, ACT.Sigmoid, tk[0], efree[i % 2])
                t = dve.tt(e, e, g, MUL, t)
                free[2 * (i % 2)] = t
                t = dve.tt(h, e, u, MUL, t, tk[1], hfree[i % 2])
                free[2 * (i % 2) + 1] = efree[i % 2] = hv[i] = t
                if i:
                    turn_h(i - 1)
                ada(1)
            turn_h(len(units) - 1)
            yb = (6, 0)
            for s, (f, w) in enumerate(tiles):
                n = w // P
                (wt,), tw, slot = slab((wd[f:f + w, :].rearrange("(p c) n -> p c n", c=n), 0, n, D))
                pe.wait(tw)
                for b in range(2):
                    pe.wait(ht[s, b])
                    if s == 0:
                        pe.wait(free[yb[b]], free[yb[b] + 1])
                    for c in range(n):
                        for h in range(2):
                            end = s == len(tiles) - 1 and c == n - 1
                            t = pe.mm(PS[:, yb[b] + h, :], HT[:, 4 * s + c, b * P:b * P + P],
                                      wt[:, c, h * 512:h * 512 + 512], s == 0 and c == 0, end,
                                      last=(c == n - 1 and h == 1))
                    if s == len(tiles) - 1:
                        free[yb[b]] = free[yb[b] + 1] = finish(b, PS[:, yb[b]:yb[b] + 2, :].rearrange("p h n -> p (h n)"), t)
                rel[slot] = t

        def project(w, n, xt):
            toks = [None, None]
            k = 0
            for f in range(0, n, 512):
                c1 = min(512, n - f)
                (wt,), tw, slot = slab((w[:, f:f + c1].rearrange("(c p) n -> p c n", p=P), 0, 8, c1))
                for b in range(2):
                    B = k % 4
                    k += 1
                    pe.wait(free[B], tw)
                    for c in range(8):
                        t = pe.mm(PS[:, B, 0:c1], XT[:, c, b * P:b * P + P], wt[:, c, :], c == 0, c == 7, xt[c],
                                  last=(c == 7))
                    if b == 1:
                        rel[slot] = t
                    dst = PR[:, b * 2304 + f:b * 2304 + f + c1]
                    if b == 0:
                        free[B] = toks[b] = sca.cp(dst, PS[:, B, 0:c1], t)
                    else:
                        free[B] = toks[b] = dve.cp(dst, PS[:, B, 0:c1], t)
            return toks

        PRB = PR[:, :].rearrange("p (b n) -> p b n", b=2)

        def heads(lo, n):
            return PRB[:, :, lo:lo + n * 64].rearrange("p b (h d) -> p b h d", d=64)

        def norm_heads(x, n, np_, nb, dd, sq, ss, gain, *w):
            t = dve.tt(sq, x, x, MUL, *w)
            t = dve.red(ss, sq, ADD, t)
            m = SM[0:np_, 168:168 + nb * n].rearrange("p (b h) -> p b h", b=nb)
            t = dve.ts(m, ss, 1.0 / dd, EPS, MUL, ADD, t)
            t = dve.rsqrt(ss, m, SM[0:np_, 184:184 + nb * n].rearrange("p (b h) -> p b h", b=nb), t)
            sh = [np_, nb, n, dd]
            t = dve.tt(x, x, bc(ss, sh, (3,)), MUL, t)
            for b in range(nb):
                t2 = dve.tt(x[:, b], x[:, b], bc(gain, [np_, n, dd], (1,)), MUL, t)
            return t2

        def rope8(x, n, np_, slot, a, b, *w):
            v = x[:, :, 0:16].rearrange("p h (t j) -> p h t j", t=2)
            sh = [np_, n, 2, 8]
            ta = dve.tt(a, v, bc(CS[0:np_, 0, slot, :], sh, (1, 1)), MUL, *w)
            tb = dve.tt(b, v, bc(CS[0:np_, 1, slot, :], sh, (1, 1)), MUL, *w)
            dve.tt(v[:, :, 0, :], a[:, :, 0, :], b[:, :, 1, :], SUB, ta, tb)
            return dve.tt(v[:, :, 1, :], a[:, :, 1, :], b[:, :, 0, :], ADD, ta, tb)

        kz_pair = [None]

        class Attn:

            def __init__(self):
                self.i = 0
                self.todo = None
                self.pfree = [None, None]
                self.tfree = [None, None]

            def group(self, nk, scores, soft, values):
                i = self.i
                self.i += 1
                s0 = 2 * (i % 2)
                pe.wait(free[s0], free[s0 + 1])
                t = scores(s0)
                tp = soft(s0, i, t, self.pfree[i % 2])
                free[s0] = free[s0 + 1] = tp
                self.flush()
                self.todo = (i, nk, tp, values)

            def flush(self):
                if self.todo is None:
                    return
                i, nk, tp, values = self.todo
                self.todo = None
                te = []
                pe.wait(tp, self.tfree[i % 2])
                kp = min(nk, P)
                nh = 4 if nk > 15 else 8
                for kc in range(max(1, nk // P)):
                    for j in range(nh if nk > 15 else 4):
                        B = 4 + kc
                        src = PB[:, i % 2, j * 256 + kc * P:j * 256 + kc * P + kp]
                        t = pe.tr(PS[0:kp, B, j * P:j * P + P], src, ident, free[B], last=(j == 3))
                    dst = PTB[0:kp, i % 2, kc * 512:kc * 512 + 512]
                    k = (dve if kc == 0 else sca).cp(dst, PS[0:kp, B, 0:512], t, self.tfree[i % 2])
                    free[B] = k
                    te.append(k)
                self.pfree[i % 2] = t
                self.tfree[i % 2] = values(i, te)

        HP = M2[:, 0:1144].rearrange("p (c n) -> p c n", c=4)
        Y = M2[:, 1144:2168].rearrange("p (c n) -> p c n", c=4)
        CB = M2[:, 2168:2648].rearrange("p (m n) -> p m n", n=30)
        KVT = M2[:, 2648:3160].rearrange("p (k n) -> p k n", k=2)
        HB = M2[:, 3160:3340]
        KC15 = M2[:, 3340:3468]
        VC15 = M2[:, 3468:3596]
        KZC = SM[:, 200:264]

        def mix_first(l):
            xt = norm_turn(lambda c: vcol("attn_norm_g", l, c), None)
            W = A["w_in"][l]
            tz = pool.ms(KZ[:, :], 0.0, *xtok)
            tz = pool.ms(HP[:, :, 0:30], 0.0, *xtok)
            tz = pool.ms(KZC, 0.0, *xtok)
            tp = project(W, 1304, xt)
            gt = SM[:, 16:64].rearrange("p (b n) -> p b n", b=2)
            tg = sca.act(gt, PRB[:, :, 1280:1304], ACT.Sigmoid, *tp)
            sl = [slab((W[:, f:f + 512].rearrange("(c p) n -> p c n", p=P), 0, 8, 512)) for f in (1304, 1816)]
            thp = []
            for ch in range(4):
                B = ch
                pe.wait(free[B], sl[0][1], sl[1][1])
                for q in range(2):
                    for c in range(8):
                        t = pe.mm(PS[:, B, q * 256:q * 256 + 256], sl[q][0][0][:, c, ch * P:ch * P + P], XT[:, c, :],
                                  c == 0, c == 7, last=(c == 7 and q == 1))
                e = TMP[:, 3072 + 256 * ch:3072 + 256 * ch + 256]
                k = sca.act(e, PS[:, B, 256:512], ACT.Sigmoid, t)
                k = dve.tt(HP[:, ch, 30:286], e, PS[:, B, 0:256], MUL, k, tz)
                free[B] = k
                thp.append(k)
            rel[sl[0][2]] = rel[sl[1][2]] = t

            def conv():
                ct = [None] * 4
                for k in range(31):
                    for ch in range(4):
                        h, w = HP[:, ch, k:k + 256], CW[:, 4 * l + ch, k:k + 1]
                        if k == 0:
                            ct[ch] = dve.ts(Y[:, ch, :], h, w, vcol("conv_b", l, ch, 4), MUL, ADD, thp[ch], tvc)
                        else:
                            ct[ch] = dve.stt(Y[:, ch, :], h, w, Y[:, ch, :], MUL, ADD, ct[ch])
                        yield ct
            cv = conv()
            cvt = [None]

            def step(n):
                for _ in range(n):
                    r = next(cv, None)
                    if r is None:
                        return False
                    cvt[0] = r
                return True

            ss = SM[:, 64:100].rearrange("p (b h) -> p b h", b=2)
            tq = [None, None]
            for lo, n, gi, so in ((0, 8, 0, 0), (768, 2, 2, 8), (1024, 2, 3, 10)):
                x = heads(lo, n)
                sq = TMP[:, 0:2 * n * 64].rearrange("p (b h d) -> p b h d", b=2, d=64)
                t = norm_heads(x, n, P, 2, 64, sq, ss[:, :, so:so + n], QKG[:, l, gi, :], *tp, tsm, *tq)
                ra = TMP[:, 1024:1024 + n * 16].rearrange("p (h t j) -> p h t j", t=2, j=8)
                rb = TMP[:, 1280:1280 + n * 16].rearrange("p (h t j) -> p h t j", t=2, j=8)
                for b in range(2):
                    tq[b] = rope8(x[:, b], n, P, b, ra, rb, t, trope, *tq)
            for b in range(2):
                pe.wait(free[4 + b], tq[b])
                for pr in range(4):
                    t = pe.tr(PS[:, 4 + b, pr * P:pr * P + P], PRB[:, b, pr * P:pr * P + P], ident, last=(pr == 3))
                free[4 + b] = tqt = sca.cp(QT[:, 0:4, b * P:b * P + P],
                                           PS[:, 4 + b, :].rearrange("p (c n) -> p c n", c=4), t)
            KZ1 = KZ[:, 0:2048].rearrange("p (k v r n) -> p k v r n", k=2, v=2, r=2)
            tk = None

            def swap(dst, src, np_, *w):
                dve.cp(dst[:, 0:64], src[:, 64:128], *w)
                return dve.cp(dst[:, 64:128], src[:, 0:64], *w)

            SW = TMP[:, 1536:2048].rearrange("p (k b n) -> p k b n", k=2, b=2)
            tsw = {}
            for k, lo in ((0, 768), (1, 1024)):
                for b in range(2):
                    tsw[k, b] = swap(SW[:, k, b, :], PRB[:, b, lo:lo + P], P, tq[b])
            for k, lo in ((0, 768), (1, 1024)):
                B = 6 + k
                pe.wait(free[B])
                for b in range(2):
                    pe.tr(PS[:, B, b * P:b * P + P], PRB[:, b, lo:lo + P], ident, tsw[k, b])
                    t = pe.tr(PS[:, B, 256 + b * P:256 + b * P + P], SW[:, k, b, :], ident, last=(b == 1))
                dve.cp(KZ1[0:64, k, 0, 0, :], PS[0:64, B, 0:256], t, tz)
                dve.cp(KZ1[64:128, k, 1, 1, :], PS[64:128, B, 0:256], t)
                dve.cp(KZ1[0:64, k, 1, 0, :], PS[0:64, B, 256:512], t)
                free[B] = tk = dve.cp(KZ1[64:128, k, 0, 1, :], PS[64:128, B, 256:512], t)
            (w1k, w1v), tw, slot = slab((A["cmp_w1_k"][l].rearrange("(m p) h -> p m h", p=P), 0, 16, P),
                                        (A["cmp_w1_v"][l].rearrange("(m p) h -> p m h", p=P), 2048, 16, P))
            tcb = None
            for q, (w1, lo, dst) in enumerate(((w1k, 512, KC15), (w1v, 640, VC15))):
                pe.wait(free[6], *tp)
                for v in range(2):
                    for b in range(2):
                        t = pe.tr(PS[0:64, 6, v * 256 + b * P:v * 256 + b * P + P],
                                  PRB[:, b, lo + v * 64:lo + v * 64 + 64], ident, last=(v == 1 and b == 1))
                src = PS[0:64, 6, :].rearrange("p (n t) -> p t n", t=2)
                kt = KVT[:, 0, :]
                dve.cp(kt[0:64, :], src[:, 0, :], t, tcb)
                free[6] = t = dve.cp(kt[64:128, :], src[:, 1, :], t, tcb)
                ktv = kt.rearrange("p (v n) -> p v n", v=2)
                tile, r = VAT[("cmp_pos_k", "cmp_pos_v")[q], l]
                for m in range(16):
                    o = CB[:, m, :].rearrange("p (v n) -> p v n", v=2)
                    k = dve.ts(o, ktv[:, :, m:m + 113:8], VC[:, tile, r + m:r + m + 1], None, ADD, None, t, tvc, tcb)
                pe.wait(k, tw, free[7])
                for m in range(16):
                    t = pe.mm(PS[:, 7, 0:30], w1[:, m, :], CB[:, m, :], m == 0, m == 15, last=(m == 15))
                tcb = t
                x = HB[:, 0:30]
                t = dve.cp(x, PS[:, 7, 0:30], t)
                free[7] = t
                u = HB[:, 30:60]
                t = dve.tt(u, x, x, MUL, t)
                t = dve.ts(u, u, 0.044715, 1.0, MUL, ADD, t)
                t = dve.tt(u, u, x, MUL, t)
                t = sca.act(u, u, ACT.Sigmoid, t, scale=2.0 * 0.7978845608028654)
                t = dve.tt(u, x, u, MUL, t)
                pe.wait(t, free[7])
                for v in range(2):
                    t = pe.mm(PS[0:NCMP, 7, v * 64:v * 64 + 64], u[:, v * 15:v * 15 + 15], W2[:, 2 * l + q, :],
                              True, True, last=(v == 1))
                free[7] = tcv = dve.cp(dst[0:NCMP, :], PS[0:NCMP, 7, 0:128], t)
                if q == 0:
                    xk = KC15[0:NCMP, :].rearrange("p (b h d) -> p b h d", b=1, d=64)
                    sq = HB[0:NCMP, 30:158].rearrange("p (b h d) -> p b h d", b=1, d=64)
                    t = norm_heads(xk, 2, NCMP, 1, 64, sq, SM[0:NCMP, 100:102].rearrange("p (b h) -> p b h", b=1),
                                   QKG[0:NCMP, l, 1, :], tcv)
                    ra = SM[0:NCMP, 104:136].rearrange("p (h t j) -> p h t j", t=2, j=8)
                    rb = SM[0:NCMP, 136:168].rearrange("p (h t j) -> p h t j", t=2, j=8)
                    tkc = rope8(xk[:, 0], 2, NCMP, 2, ra, rb, t, trope)
            rel[slot] = tcb
            sw = HB[0:NCMP, 30:158]
            t = swap(sw, KC15[0:NCMP, :], NCMP, tkc)
            pe.wait(t, free[6])
            pe.tr(PS[:, 6, 0:NCMP], KC15[0:NCMP, :], ident[0:NCMP, 0:NCMP])
            t = pe.tr(PS[:, 6, 16:16 + NCMP], sw, ident[0:NCMP, 0:NCMP], last=True)
            KC = KZC.rearrange("p (v r n) -> p v r n", v=2, r=2)
            dve.cp(KC[0:64, 0, 0, 0:15], PS[0:64, 6, 0:15], t, tz)
            dve.cp(KC[64:128, 1, 1, 0:15], PS[64:128, 6, 0:15], t)
            dve.cp(KC[0:64, 1, 0, 0:15], PS[0:64, 6, 16:31], t)
            free[6] = tkc = dve.cp(KC[64:128, 0, 1, 0:15], PS[64:128, 6, 16:31], t)

            at = Attn()
            oa = [None, None]
            obank = {}
            gv = gt.rearrange("p b (h r) -> p b r h", r=3)
            nob = [0]

            def one(b, kind, v):
                nk = NCMP if kind == 0 else P * (b + 1)
                so = 264 + 8 * ((b * 3 + kind) * 2 + v)
                mx, sm = SM[:, so:so + 4], SM[:, so + 4:so + 8]

                def scores(s0):
                    pe.wait(tqt, tk, tkc)
                    for j in range(4):
                        h = 4 * v + j
                        rhs = KC[:, v, j % 2, 0:15] if kind == 0 else KZ1[:, kind - 1, v, j % 2, 0:nk]
                        t = pe.mm(PS[:, s0 + j // 2, (j % 2) * 256:(j % 2) * 256 + nk],
                                  QT[:, h // 2, b * P:b * P + P], rhs, True, True, last=(j == 3))
                    return t

                def soft(s0, i, t, pf):
                    s4 = PS[:, s0:s0 + 2, :].rearrange("p k (j n) -> p (k j) n", j=2)
                    if kind == 0:
                        dg, mk = s4[:, :, 0:15], C[:, CM + 15 * b:CM + 15 * b + 15]
                    else:
                        dg, mk = s4[:, :, nk - P:nk], C[:, CC:CC + P]
                    t = dve.tt(dg, dg, bc(mk, [P, 4, min(nk, P)], (1,)), ADD, t)
                    t = dve.red(mx, s4[:, :, 0:nk], MAX, t, neg=True)
                    t = dve.ts(mx, mx, 0.125, None, MUL, None, t)
                    for j in range(4):
                        te = sca.act(PB[:, i % 2, j * 256:j * 256 + nk], s4[:, j, 0:nk], ACT.Exp, t, pf,
                                     bias=mx[:, j:j + 1], scale=0.125, acc=sm[:, j:j + 1])
                    k = dve.rcp(sm, sm, te)
                    k = dve.tt(sm, sm, gv[:, b, kind, 4 * v:4 * v + 4], MUL, k, tg)
                    if kind == 0:
                        k = dve.ts(sm, sm, C[:, CV + b:CV + b + 1], None, MUL, None, k)
                    obank[b, kind, v] = k
                    step(10)
                    return te

                def values(i, te):
                    if v == 0:
                        nob[0] += 1
                    B = 6 + nob[0] % 2
                    pe.wait(*te)
                    if v == 0:
                        pe.wait(free[B])
                    kp = min(nk, P)
                    nkc = max(1, nk // P)
                    for j in range(4):
                        h = 4 * v + j
                        for kc in range(nkc):
                            if kind == 0:
                                vv = VC15[0:NCMP, v * 64:v * 64 + 64]
                            else:
                                vv = PRB[:, kc, 640 + 256 * kind + v * 64:640 + 256 * kind + v * 64 + 64]
                            t = pe.mm(PS[:, B, h * 64:h * 64 + 64], PTB[0:kp, i % 2, kc * 512 + j * P:kc * 512 + j * P + P],
                                      vv, kc == 0, kc == nkc - 1, last=(j == 3 and kc == nkc - 1))
                    if v == 1:
                        o3 = PS[:, B, :].rearrange("p (v h d) -> p v h d", v=2, d=64)
                        acc = OA[:, b, :].rearrange("p (v h d) -> p v h d", v=2, d=64)
                        tmp = TMPO.rearrange("p (v h d) -> p v h d", v=2, d=64)
                        for vv in range(2):
                            so_ = 264 + 8 * ((b * 3 + kind) * 2 + vv) + 4
                            cf = bc(SM[:, so_:so_ + 4], [P, 4, 64], (2,))
                            if kind == 0:
                                oa[b] = free[B] = dve.tt(acc[:, vv], o3[:, vv], cf, MUL, t, obank[b, kind, vv])
                            else:
                                free[B] = k = dve.tt(tmp[:, vv], o3[:, vv], cf, MUL, t, obank[b, kind, vv], oa[b])
                        if kind:
                            oa[b] = dve.tt(OA[:, b, :], OA[:, b, :], TMPO, ADD, k)
                    return t

                at.group(nk, scores, soft, values)

            TMPO = GB[:, 0:512]
            for b in range(2):
                for kind in range(3):
                    for v in range(2):
                        one(b, kind, v)
            at.flush()
            while step(8):
                pass
            B = 0
            pe.wait(free[0], *cvt[0])
            for ch in range(4):
                t = pe.mm(PS[:, 0, 0:256], ones, Y[:, ch, :], ch == 0, ch == 3, last=(ch == 3))
            mean = TMP[:, 0:256]
            free[0] = t = sca.act(mean, PS[:, 0, 0:256], ACT.Copy, t, *at.tfree, scale=1.0 / 512)
            SQ = TMP[:, 1024:2048].rearrange("p (c n) -> p c n", c=4)
            yc = dve.tt(Y[:, :, :], Y[:, :, :], bc(mean, [P, 4, 256], (1,)), SUB, t)
            t = sca.act(SQ, Y[:, :, :], ACT.Square, yc)
            pe.wait(t, free[1])
            for ch in range(4):
                t = pe.mm(PS[:, 1, 0:256], ones, SQ[:, ch, :], ch == 0, ch == 3, last=(ch == 3))
            rs = TMP[:, 256:512]
            free[1] = t = dve.ts(rs, PS[:, 1, 0:256], 1.0 / 512, EPS, MUL, ADD, t)
            rs2 = TMP[:, 512:768]
            t = dve.rsqrt(rs2, rs, TMP[:, 768:1024], t)
            rs = rs2
            t = dve.tt(Y[:, :, :], Y[:, :, :], bc(rs, [P, 4, 256], (1,)), MUL, t)
            for ch in range(4):
                k = dve.ts(Y[:, ch, :], Y[:, ch, :], vcol("conv_ln_g", l, ch, 4), vcol("conv_ln_b", l, ch, 4), MUL, ADD, t)
            t = sca.act(SQ, Y[:, :, :], ACT.Sigmoid, k)
            tconv = dve.tt(MT[:, 4:8, :], Y[:, :, :], SQ, MUL, t)
            for b in range(2):
                B = 2 + b
                pe.wait(free[B], oa[b])
                for c in range(4):
                    t = pe.tr(PS[:, B, c * P:c * P + P], OA[:, b, c * P:c * P + P], ident, last=(c == 3))
                free[B] = toa = sca.cp(MT[:, 0:4, b * P:b * P + P], PS[:, B, :].rearrange("p (c n) -> p c n", c=4), t)
            for h in range(2):
                (wt,), tw, slot = slab((A["w_out"][l][:, h * 512:h * 512 + 512].rearrange("(c p) n -> p c n", p=P),
                                        0, 8, 512))
                for b in range(2):
                    B = 4 + 2 * h + b
                    pe.wait(free[B], tw, tconv, toa)
                    for c in range(8):
                        t = pe.mm(PS[:, B, :], MT[:, c, b * P:b * P + P], wt[:, c, :], c == 0, c == 7, last=(c == 7))
                    xh = X[:, b, h * 512:h * 512 + 512]
                    free[B] = xtok[b] = dve.tt(xh, xh, PS[:, B, :], ADD, t)
                rel[slot] = t

        def ffn_first():
            xt = norm_turn(lambda c: vcol("ffn_norm_g", 0, c), None)

            def finish(b, y, t):
                xtok[b] = dve.tt(X[:, b, :], X[:, b, :], y, ADD, t)
                return xtok[b]
            swiglu(xt, F1, A["ffn_w_gate"][0], A["ffn_w_up"][0], A["ffn_w_down"][0], finish)

        def moe():
            xt = norm_turn(lambda c: vcol("ffn_norm_g", 1, c), None)
            tile, r = VAT["ffn_norm_g"]
            gain = VC[:, tile, r + 8:r + 16]
            GW = SM[:, 16:32].rearrange("p (b e) -> p b e", b=2)
            M = SM[:, 80:96].rearrange("p (b e) -> p b e", b=2)
            RK = SM[:, 96:112].rearrange("p (b e) -> p b e", b=2)
            t = None
            for b in range(2):
                pe.wait(free[b])
                for c in range(8):
                    t = pe.mm(PS[:, b, 0:8], XT[:, c, b * P:b * P + P], RT[:, c, :], c == 0, c == 7, xt[c],
                              last=(c == 7))
                lg, m8, gg = SM[:, 32:40], SM[:, 40:48], SM[:, 48:52]
                ix, fx, oh = SM[:, 56:64].bitcast(U32), SM[:, 64:72], SM[:, 72:80]
                free[b] = t = dve.cp(lg, PS[:, b, 0:8], t)
                t = dve.inc(lambda e: e.max(m8, lg), t)
                t = dve.inc(lambda e: e.max_index(ix, m8, lg), t)
                t = dve.cp(fx, ix, t)
                t = dve.tt(gg[:, 0:1], m8[:, 1:2], m8[:, 0:1], SUB, t)
                sca.act(gg[:, 2:3], gg[:, 0:1], ACT.Sigmoid, t, scale=-1.0)
                t = sca.act(gg[:, 3:4], gg[:, 0:1], ACT.Sigmoid, t)
                io = C[:, CR:CR + 8]
                t = dve.ts(GW[:, b, :], io, fx[:, 0:1], gg[:, 2:3], ALU.is_equal, MUL, t)
                t = dve.ts(oh, io, fx[:, 1:2], gg[:, 3:4], ALU.is_equal, MUL, t)
                t = dve.tt(GW[:, b, :], GW[:, b, :], oh, ADD, t)
                t = dve.ts(M[:, b, :], io, fx[:, 0:1], None, ALU.is_equal, None, t)
                t = dve.ts(oh, io, fx[:, 1:2], None, ALU.is_equal, None, t)
                t = dve.tt(M[:, b, :], M[:, b, :], oh, ADD, t)
            pe.wait(t, free[2], free[3])
            pe.mm(PS[:, 2, 0:8], C[:, CT:CT + P], M[:, 0, :], True, True)
            pe.mm(PS[:, 2, 8:16], C[:, CT:CT + P], M[:, 1, :], True, False)
            t = pe.mm(PS[:, 2, 8:16], ones, M[:, 0, :], False, True, last=True)
            pe.mm(PS[:, 3, 0:8], ones, M[:, 0, :], True, False)
            t2 = pe.mm(PS[:, 3, 0:8], ones, M[:, 1, :], False, True, last=True)
            k = dve.ts(RK, M, -1000.0, 1000.0, MUL, ADD, t)
            free[2] = trk = dve.tt(RK, RK, PS[:, 2, 0:16].rearrange("p (b e) -> p b e", b=2), ADD, k)
            most = SM[:, 120:121]
            free[3] = k = dve.red(most, PS[:, 3, 0:8], MAX, t2)
            tmost = dve.cp(MOSTI[:, :], most, k)

            XE = MT[:, :, :].rearrange("p a n -> p (a n)").rearrange("p (k c n) -> p k c n", k=2, c=8)
            HM = R[:, 0:1024].rearrange("p (k n) -> p k n", k=2)
            YS = R[:, 1024:3072].rearrange("p (k n) -> p k n", k=2)
            PG = M2[:, 0:256].rearrange("p (b n) -> p b n", b=2)
            PW = M2[:, 256:512].rearrange("p (b n) -> p b n", b=2)
            PT = M2[:, 512:1024].rearrange("p (k n) -> p k n", k=2)
            g3 = bc(gain, [P, 8, P], (2,))

            def choose(d, pw, pg, io, e, *w):
                for b in range(2):
                    d.ts(pg[:, b, :], io, RK[:, b, e:e + 1], None, ALU.is_equal, None, trk, *w)
                    t = d.ts(pw[:, b, :], io, RK[:, b, e:e + 1], GW[:, b, e:e + 1], ALU.is_equal, MUL)
                return t

            txe, tpt, tys = {}, {}, {}
            pgfree = [None]

            def turn_p(e):
                B = 4 + 2 * (e % 2)
                t = choose(dve, PW, PG, C[:, CR:CR + P], e, pgfree[0])
                pe.wait(t, free[B])
                for b in range(2):
                    t = pe.tr(PS[:, B, b * P:b * P + P], PW[:, b, :], ident, last=(b == 1))
                free[B] = tpt[e] = sca.cp(PT[:, e % 2, :], PS[:, B, 0:256], t)

            def gather(e):
                B = 4 + 2 * (e % 2)
                for k in range(2):
                    pe.wait(free[B + k])
                    for c in range(4):
                        for b in range(2):
                            t = pe.mm(PS[:, B + k, c * P:c * P + P], XS[:, b, (4 * k + c) * P:(4 * k + c) * P + P],
                                      PG[:, b, :], b == 0, b == 1, last=(c == 3 and b == 1))
                    free[B + k] = txe[e, k] = dve.tt(XE[:, e % 2, 4 * k:4 * k + 4, :],
                                                     PS[:, B + k, :].rearrange("p (c n) -> p c n", c=4),
                                                     g3[:, 4 * k:4 * k + 4, :], MUL, t)
                pgfree[0] = t

            def save_y(e, t):
                B = 4 + 2 * (e % 2)
                k = sca.cp(YS[:, e % 2, :], PS[:, B:B + 2, :].rearrange("p h n -> p (h n)"), t)
                free[B] = free[B + 1] = tys[e] = k

            def scatter(e, b):
                B = 4 + 2 * (e % 2)
                pe.wait(free[B], free[B + 1], tys[e], tpt[e])
                for h in range(2):
                    t = pe.mm(PS[:, B + h, :], PT[:, e % 2, b * P:b * P + P], YS[:, e % 2, h * 512:h * 512 + 512],
                              True, True, last=(h == 1))
                xtok[b] = dve.tt(X[:, b, :], X[:, b, :], PS[:, B:B + 2, :].rearrange("p h n -> p (h n)"), ADD, t, xtok[b])
                free[B] = free[B + 1] = xtok[b]

            units = [(e, s) for e in range(NE) for s in range(7)]
            hv, ht, hfree, efree = {}, {}, [None, None], [None, None]

            def down(i):
                e, s = units[i]
                f = 512 * s
                (wt,), tw, slot = slab((A["moe_w_down"][0, e][f:f + 512, :].rearrange("(p c) n -> p c n", c=4), 0, 4, D))
                B = 4 + 2 * (e % 2)
                pe.wait(tw, ht[i])
                if s == 0:
                    pe.wait(free[B], free[B + 1])
                for c in range(4):
                    for h in range(2):
                        t = pe.mm(PS[:, B + h, :], HM[:, i % 2, c * P:c * P + P], wt[:, c, h * 512:h * 512 + 512],
                                  s == 0 and c == 0, s == 6 and c == 3, last=(c == 3 and h == 1))
                rel[slot] = t
                if s == 6:
                    save_y(e, t)

            def turn_h(i):
                B = 2 * (i % 2)
                h = EH[:, 1, i % 2, :].rearrange("p (m c) -> p c m", c=4)
                pe.wait(free[B], hv[i])
                for c in range(4):
                    t = pe.tr(PS[:, B, c * P:c * P + P], h[:, c, :], ident, last=(c == 3))
                hfree[i % 2] = t
                ht[i] = free[B] = sca.cp(HM[:, i % 2, :], PS[:, B, :], t)

            turn_p(0)
            gather(0)
            for i, (e, s) in enumerate(units):
                f = 512 * s
                tk = []
                for B, a in ((2 * (i % 2), A["moe_w_gate"]), (2 * (i % 2) + 1, A["moe_w_up"])):
                    (wt,), tw, slot = slab((a[0, e][:, f:f + 512].rearrange("(c p) n -> p c n", p=P), 0, 8, 512))
                    pe.wait(free[B], tw)
                    for c in range(8):
                        t = pe.mm(PS[:, B, :], XE[:, e % 2, c, :], wt[:, c, :], c == 0, c == 7, txe[e, c // 4],
                                  last=(c == 7))
                    rel[slot] = t
                    tk.append(t)
                g, u = PS[:, 2 * (i % 2), :], PS[:, 2 * (i % 2) + 1, :]
                ev, h = EH[:, 0, i % 2, :], EH[:, 1, i % 2, :]
                t = sca.act(ev, g, ACT.Sigmoid, tk[0], efree[i % 2])
                t = dve.tt(ev, ev, g, MUL, t)
                free[2 * (i % 2)] = t
                t = dve.tt(h, ev, u, MUL, t, tk[1], hfree[i % 2])
                free[2 * (i % 2) + 1] = efree[i % 2] = hv[i] = t
                if i >= 1:
                    turn_h(i - 1)
                if i >= 2:
                    down(i - 2)
                if e and s in (2, 3):
                    scatter(e - 1, s - 2)
                if s == 4 and e + 1 < NE:
                    turn_p(e + 1)
                if s == 5 and e + 1 < NE:
                    gather(e + 1)
                ada(1 if (s in (3, 5) if e % 2 == 0 else s in (0, 1)) else 0)
            n = len(units)
            turn_h(n - 1)
            down(n - 2)
            down(n - 1)
            scatter(NE - 1, 0)
            scatter(NE - 1, 1)

            o_pe, o_dve, o_act = PE(sem("o_pe")), DVE(sem("o_dve")), SCA(sem("o_act"))
            s_od = sem("s_od")
            nd = [0]
            for q in (o_pe, o_dve, o_act):
                q.wait(*xtok, (pe.sem, pe.n), (sca.sem, sca.n), tmost)
            W = R[:, 0:4096]
            XO = XE[:, 0]
            HO = KZ[:, 0:512]
            YO = KZ[:, 1024:2048]
            eo, ho = EH[:, 0, 0, :], EH[:, 1, 0, :]
            last = None

            def load(src, c, *w):
                nd[0] += 16
                dst = W.rearrange("p (c n) -> p c n", c=c)
                o_act.do(lambda e: e.dma_start(dst, src).then_inc(s_od, 16), *w)
                return dst, (s_od, nd[0])

            tw_free = None
            for e in range(NE):
                t = choose(o_dve, PW, PG, C[:, CR + P:CR + 2 * P], e, last)
                o_pe.wait(t)
                for b in range(2):
                    t = o_pe.tr(PS[:, 0, b * P:b * P + P], PW[:, b, :], ident, last=(b == 1))
                tpo = o_dve.cp(PT[:, 0, :], PS[:, 0, 0:256], t)
                for k in range(2):
                    for c in range(4):
                        for b in range(2):
                            t = o_pe.mm(PS[:, 1 + k, c * P:c * P + P], XS[:, b, (4 * k + c) * P:(4 * k + c) * P + P],
                                        PG[:, b, :], b == 0, b == 1, last=(c == 3 and b == 1))
                    txo = o_dve.tt(XO[:, 4 * k:4 * k + 4, :], PS[:, 1 + k, :].rearrange("p (c n) -> p c n", c=4),
                                   g3[:, 4 * k:4 * k + 4, :], MUL, t)
                for s in range(7):
                    f = 512 * s
                    for B, a in ((3, A["moe_w_gate"]), (4, A["moe_w_up"])):
                        wt, tw = load(a[0, e][:, f:f + 512].rearrange("(c p) n -> p c n", p=P), 8, tw_free)
                        o_pe.wait(tw, txo)
                        for c in range(8):
                            t = o_pe.mm(PS[:, B, :], XO[:, c, :], wt[:, c, :], c == 0, c == 7, last=(c == 7))
                        tw_free = t
                    k = o_act.act(eo, PS[:, 3, :], ACT.Sigmoid, t)
                    k = o_dve.tt(eo, eo, PS[:, 3, :], MUL, k)
                    k = o_dve.tt(ho, eo, PS[:, 4, :], MUL, k)
                    o_pe.wait(k)
                    hc = ho.rearrange("p (m c) -> p c m", c=4)
                    for c in range(4):
                        t = o_pe.tr(PS[:, 5, c * P:c * P + P], hc[:, c, :], ident, last=(c == 3))
                    k = o_dve.cp(HO, PS[:, 5, :], t)
                    wt, tw = load(A["moe_w_down"][0, e][f:f + 512, :].rearrange("(p c) n -> p c n", c=4), 4, tw_free)
                    o_pe.wait(tw, k)
                    for c in range(4):
                        for h in range(2):
                            t = o_pe.mm(PS[:, 6 + h, :], HO[:, c * P:c * P + P], wt[:, c, h * 512:h * 512 + 512],
                                        s == 0 and c == 0, s == 6 and c == 3, last=(c == 3 and h == 1))
                    tw_free = t
                k = o_dve.cp(YO, PS[:, 6:8, :].rearrange("p h n -> p (h n)"), t)
                o_pe.wait(k, tpo)
                for b in range(2):
                    for h in range(2):
                        t = o_pe.mm(PS[:, 4 * b + h, :], PT[:, 0, b * P:b * P + P], YO[:, h * 512:h * 512 + 512],
                                    True, True, last=(h == 1))
                    last = o_dve.tt(X[:, b, :], X[:, b, :], PS[:, 4 * b:4 * b + 2, :].rearrange("p h n -> p (h n)"),
                                    ADD, t, last)
                o_pe.wait(last)
            for q in (o_pe, o_dve, o_act):
                q.wait(last, (o_act.sem, o_act.n))

            def branch(q, body):
                def f(e):
                    most = e.value_load(MOSTI[0:1, 0:1], min_val=0, max_val=S)
                    with e.If(most > CAP):
                        body.run(e)
                q.do(f, tmost)

            branch(pe, o_pe)
            branch(dve, o_dve)
            branch(sca, o_act)
            xtok[0] = xtok[1] = dve.cp(SM[:, 121:122], SM[:, 120:121])

        def gate_rows(l, k, half):
            for h in range(2):
                B = 4 + h
                pe.wait(free[B], ada_tok[l])
                for c in range(4):
                    g = MODC[:, l, 8 * k + 4 * h + c:8 * k + 4 * h + c + 1].to_broadcast([P, P])
                    t = pe.mm(PS[:, B, c * P:c * P + P], g, ident, True, True, last=(c == 3))
                free[B] = t = sca.act(GB[:, h * 512:h * 512 + 512], PS[:, B, :], ACT.Copy, t, *xtok,
                                      scale=0.5 if half else 1.0)
            return t


        def norm_mod(l, k):
            g = VC[:, VAT["norm_g_2"][0], VAT["norm_g_2"][1] + (l * 3 + k) * 8:VAT["norm_g_2"][1] + (l * 3 + k) * 8 + 8]
            sc = SM[:, 8:16]
            t = dve.stt(sc, MODC[:, l, (3 * k + 1) * 8:(3 * k + 2) * 8], 1.0, g, ADD, MUL, ada_tok[l])
            return norm_turn(lambda c: sc[:, c:c + 1], lambda c: MODC[:, l, 3 * k * 8 + c:3 * k * 8 + c + 1], t)

        def ffn_second(l, i):
            xt = norm_mod(l, 2 * i)
            tg = gate_rows(l, 6 * i + 2, True)
            T = M2[:, 0:1024]

            def finish(b, y, t):
                k = dve.tt(T, y, GB[:, :], MUL, t, tg, *xtok)
                xtok[b] = dve.tt(X[:, b, :], X[:, b, :], T, ADD, k)
                return xtok[b]
            swiglu(xt, F2, A["ffn_wg_2"][l, i], A["ffn_wu_2"][l, i], A["ffn_wd_2"][l, i], finish)

        def mix_second(l):
            lam_init = 0.8 - 0.6 * float(np.exp(-0.3 * l))
            xt = norm_mod(l, 1)
            tgb = gate_rows(l, 5, False)
            tz = pool.ms(KZ[:, :], 0.0, *xtok)
            tp = project(A["w_in_2"][l], 2304, xt)
            lp = LP[:, l, :].rearrange("p (a d) -> p a d", d=64)
            lt, lv = SM[:, 16:144].rearrange("p (a d) -> p a d", d=64), SM[:, 144:146]
            t = dve.tt(lt, lp[:, 0::2, :], lp[:, 1::2, :], MUL, tsm)
            t = dve.red(lv, lt, ADD, t)
            t = sca.act(lv, lv, ACT.Exp, t)
            nlam = SM[:, 146:147]
            t = dve.tt(nlam, lv[:, 1:2], lv[:, 0:1], SUB, t)
            tlam = dve.ts(nlam, nlam, -lam_init, None, ADD, None, t)
            tq = [None, None]
            for lo, n, gi, so in ((0, 8, 0, 0), (512, 2, 1, 8)):
                x = heads(lo, n)
                sq = TMP[:, 0:2 * n * 64].rearrange("p (b h d) -> p b h d", b=2, d=64)
                ss = SM[:, 64:84].rearrange("p (b h) -> p b h", b=2)[:, :, so:so + n]
                t = norm_heads(x, n, P, 2, 64, sq, ss, QG2[:, l, gi, :], *tp, tsm, tlam, *tq)
                m = 2 * n
                ra = TMP[:, 1024:1024 + n * 64].rearrange("p (m s j) -> p m s j", s=2, j=32)
                rb = TMP[:, 1536:1536 + n * 64].rearrange("p (m s j) -> p m s j", s=2, j=32)
                for b in range(2):
                    cs = C[:, CA + 64 * b:CA + 64 * b + 64].rearrange("p (q s j) -> p q s j", q=2, j=16)
                    for s in range(2):
                        v = x[:, b, :, 32 * s:32 * s + 32].rearrange("p h (t j) -> p h t j", t=2)
                        a_ = ra[:, 0:n, s, :].rearrange("p h (t j) -> p h t j", t=2)
                        b_ = rb[:, 0:n, s, :].rearrange("p h (t j) -> p h t j", t=2)
                        sh = [P, n, 2, 16]
                        ta = dve.tt(a_, v, bc(cs[:, 0, s, :], sh, (1, 1)), MUL, t, tq[s])
                        tb = dve.tt(b_, v, bc(cs[:, 1, s, :], sh, (1, 1)), MUL, t, tq[s])
                        dve.tt(v[:, :, 0, :], a_[:, :, 0, :], b_[:, :, 1, :], SUB, ta, tb)
                        tq[b] = dve.tt(v[:, :, 1, :], a_[:, :, 1, :], b_[:, :, 0, :], ADD, ta, tb)
            tqa = tq[1]
            for k, lo in ((0, 0), (1, 768)):
                for b in range(2):
                    B = 4 + b
                    pe.wait(free[B], tqa, *tp)
                    for pr in range(4):
                        t = pe.tr(PS[:, B, pr * P:pr * P + P], PRB[:, b, lo + pr * P:lo + pr * P + P], ident,
                                  last=(pr == 3))
                    free[B] = tqt = sca.cp(QT[:, 4 * k:4 * k + 4, b * P:b * P + P],
                                           PS[:, B, :].rearrange("p (c n) -> p c n", c=4), t)
            KA = KZ[:, 0:1024].rearrange("p (v r n) -> p v r n", v=2, r=2)
            KD = KZ[:, 1024:3072].rearrange("p (c r n) -> p c r n", c=4, r=2)
            SW = TMP[:, 2048:2304].rearrange("p (b n) -> p b n", b=2)
            for b in range(2):
                dve.cp(SW[:, b, 0:64], PRB[:, b, 576:640], tqa)
                tsw = dve.cp(SW[:, b, 64:128], PRB[:, b, 512:576], tqa)
            pe.wait(free[6], tsw)
            for b in range(2):
                pe.tr(PS[:, 6, b * P:b * P + P], PRB[:, b, 512:640], ident)
                t = pe.tr(PS[:, 6, 256 + b * P:256 + b * P + P], SW[:, b, :], ident, last=(b == 1))
            dve.cp(KA[0:64, 0, 0, :], PS[0:64, 6, 0:256], t, tz)
            dve.cp(KA[64:128, 1, 1, :], PS[64:128, 6, 0:256], t)
            dve.cp(KA[0:64, 1, 0, :], PS[0:64, 6, 256:512], t)
            free[6] = tk = dve.cp(KA[64:128, 0, 1, :], PS[64:128, 6, 256:512], t)
            for hf in range(2):
                B = 7
                pe.wait(free[B])
                for b in range(2):
                    for c in range(2):
                        t = pe.tr(PS[:, B, c * 256 + b * P:c * 256 + b * P + P],
                                  PRB[:, b, 1280 + (2 * hf + c) * P:1280 + (2 * hf + c) * P + P], ident,
                                  last=(b == 1 and c == 1))
                for c in range(2):
                    dve.cp(KD[0:64, 2 * hf + c, 0, :], PS[0:64, B, c * 256:c * 256 + 256], t)
                    free[B] = tkd = dve.cp(KD[64:128, 2 * hf + c, 1, :], PS[64:128, B, c * 256:c * 256 + 256], t)

            at = Attn()
            oa = [None, None]
            od = [None, None]
            OD = M2[:, 1024:2048].rearrange("p (b n) -> p b n", b=2)
            coef = {}

            def grouped(b, v):
                so = 264 + 8 * (b * 2 + v)
                mx, sm = SM[:, so:so + 4], SM[:, so + 4:so + 8]

                def scores(s0):
                    pe.wait(tqt, tk)
                    for j in range(4):
                        t = pe.mm(PS[:, s0 + j // 2, (j % 2) * 256:(j % 2) * 256 + 256],
                                  QT[:, (4 * v + j) // 2, b * P:b * P + P], KA[:, v, j % 2, :], True, True, last=(j == 3))
                    return t

                def soft(s0, i, t, pf):
                    s4 = PS[:, s0:s0 + 2, :].rearrange("p k (j n) -> p (k j) n", j=2)
                    t = dve.red(mx, s4, MAX, t, neg=True)
                    t = dve.ts(mx, mx, 0.125, None, MUL, None, t)
                    for j in range(4):
                        te = sca.act(PB[:, i % 2, j * 256:j * 256 + 256], s4[:, j, :], ACT.Exp, t, pf,
                                     bias=mx[:, j:j + 1], scale=0.125, acc=sm[:, j:j + 1])
                    coef[b, v] = dve.rcp(sm, sm, te)
                    return te

                def values(i, te):
                    B = 6 + b
                    pe.wait(*te)
                    if v == 0:
                        pe.wait(free[B])
                    for j in range(4):
                        h = 4 * v + j
                        for kc in range(2):
                            t = pe.mm(PS[:, B, h * 64:h * 64 + 64], PTB[:, i % 2, kc * 512 + j * P:kc * 512 + j * P + P],
                                      PRB[:, kc, 640 + v * 64:640 + v * 64 + 64], kc == 0, kc == 1,
                                      last=(j == 3 and kc == 1))
                    o4 = PS[:, B, v * 256:v * 256 + 256].rearrange("p (h d) -> p h d", d=64)
                    dst = OA[:, b, v * 256:v * 256 + 256].rearrange("p (h d) -> p h d", d=64)
                    oa[b] = dve.tt(dst, o4, bc(sm, [P, 4, 64], (2,)), MUL, t, coef[b, v])
                    if v == 1:
                        free[B] = oa[b]
                    else:
                        pe.wait(oa[b])
                    return t

                at.group(256, scores, soft, values)

            def diff(b, hp):
                so = 320 + 8 * (b * 2 + hp)
                mx, sm = SM[:, so:so + 4], SM[:, so + 4:so + 8]

                def scores(s0):
                    pe.wait(tqt, tkd)
                    for j in range(4):
                        m, r = j // 2, j % 2
                        pr = 2 * m + hp
                        t = pe.mm(PS[:, s0 + m, r * 256:r * 256 + 256], QT[:, 4 + pr, b * P:b * P + P], KD[:, pr, r, :],
                                  True, True, last=(j == 3))
                    return t

                def soft(s0, i, t, pf):
                    s4 = PS[:, s0:s0 + 2, :].rearrange("p k (j n) -> p (k j) n", j=2)
                    for r in range(2):
                        slope = 2.0 ** (-2.0 * (2 * hp + r + 1))
                        v = s4[:, r::2, :]
                        dist = bc(C[:, CD + 256 * b:CD + 256 * b + 256], [P, 2, 256], (1,))
                        t = dve.stt(v, dist, -8.0 * slope, v, MUL, ADD, t)
                    t = dve.red(mx, s4, MAX, t, neg=True)
                    t = dve.ts(mx, mx, 0.125, None, MUL, None, t)
                    e4 = PB[:, i % 2, :].rearrange("p (j n) -> p j n", j=4)
                    for j in range(4):
                        te = sca.act(e4[:, j, :], s4[:, j, :], ACT.Exp, t, pf, bias=mx[:, j:j + 1], scale=0.125,
                                     acc=sm[:, j:j + 1])
                    k = dve.rcp(sm, sm, te)
                    k = dve.ts(sm[:, 2:4], sm[:, 2:4], nlam, None, MUL, None, k, tlam)
                    for r in range(2):
                        k1 = dve.ts(e4[:, 2 + r, :], e4[:, 2 + r, :], sm[:, 2 + r:3 + r], None, MUL, None, k)
                        te = dve.stt(e4[:, r, :], e4[:, r, :], sm[:, r:r + 1], e4[:, 2 + r, :], MUL, ADD, k1)
                    return te

                def values(i, te):
                    B = 6 + b
                    pe.wait(*te)
                    if hp == 0:
                        pe.wait(free[B])
                    for r in range(2):
                        h = 2 * hp + r
                        for kc in range(2):
                            t = pe.mm(PS[:, B, h * P:h * P + P], PTB[:, i % 2, kc * 512 + r * P:kc * 512 + r * P + P],
                                      PRB[:, kc, 1792 + h * P:1792 + h * P + P], kc == 0, kc == 1,
                                      last=(r == 1 and kc == 1))
                    od[b] = dve.cp(OD[:, b, hp * 256:hp * 256 + 256], PS[:, B, hp * 256:hp * 256 + 256], t)
                    if hp == 1:
                        free[B] = od[b]
                    else:
                        pe.wait(od[b])
                    return t

                at.group(256, scores, soft, values)

            for b in range(2):
                for v in range(2):
                    grouped(b, v)
            for b in range(2):
                for hp in range(2):
                    diff(b, hp)
            at.flush()
            x = OD.rearrange("p b (h d) -> p b h d", d=P)
            sq = TMP[:, 0:1024].rearrange("p (b h d) -> p b h d", b=2, d=P)
            ss = SM[:, 64:72].rearrange("p (b h) -> p b h", b=2)
            dve.wait(*at.tfree)
            t = norm_heads(x, 4, P, 2, P, sq, ss, SG[:, l, :], *od)
            tod = dve.ts(OD, OD, 1.0 - lam_init, None, MUL, None, t)
            for k, src in ((0, OA), (1, OD)):
                for b in range(2):
                    B = 2 * k + b
                    pe.wait(free[B], oa[b], tod)
                    for c in range(4):
                        t = pe.tr(PS[:, B, c * P:c * P + P], src[:, b, c * P:c * P + P], ident, last=(c == 3))
                    free[B] = tmt = sca.cp(MT[:, 4 * k:4 * k + 4, b * P:b * P + P],
                                           PS[:, B, :].rearrange("p (c n) -> p c n", c=4), t)
            MX = QT
            bg = VAT["b_gate_2"]
            tm = None
            for q in range(4):
                f = q * 256
                (wab,), tw, slot = slab((A["w_ba_2"][l][:, f:f + 256].rearrange("(c p) n -> p c n", p=P), 0, 4, 256))
                (wbb,), tw2, slot2 = slab((A["w_bb_2"][l][:, f:f + 256].rearrange("(c p) n -> p c n", p=P), 0, 4, 256))
                (wga, wgb), tw3, slot3 = slab(
                    (A["w_gate_2"][l][:, f:f + 256].rearrange("(c p) n -> p c n", p=P), 0, 8, 256),
                    (A["w_gate_2"][l][:, D + f:D + f + 256].rearrange("(c p) n -> p c n", p=P), 2048, 8, 256))
                for cc in range(2):
                    ch = 2 * q + cc
                    B = 4 + 2 * (ch % 2)
                    o = cc * P
                    pe.wait(free[B], free[B + 1], tw, tw2, tw3, tmt)
                    for k, w in ((0, wab), (1, wbb)):
                        for c in range(4):
                            t = pe.mm(PS[:, B, k * 256:k * 256 + 256], w[:, c, o:o + P], MT[:, 4 * k + c, :], c == 0,
                                      c == 3)
                    for k, w in ((0, wga), (1, wgb)):
                        for c in range(8):
                            t = pe.mm(PS[:, B + 1, k * 256:k * 256 + 256], w[:, c, o:o + P], XT[:, c, :], c == 0,
                                      c == 7, last=(c == 7 and k == 1))
                    e = TMP[:, 1024 + 512 * (ch % 2):1536 + 512 * (ch % 2)]
                    for k in range(2):
                        col = bg[1] + l * 16 + 8 * k + ch
                        ka = sca.act(e[:, k * 256:k * 256 + 256], PS[:, B + 1, k * 256:k * 256 + 256], ACT.Sigmoid, t,
                                     tvc, tm, bias=VC[:, bg[0], col:col + 1])
                    free[B + 1] = ka
                    k = dve.tt(e, e, PS[:, B, :], MUL, ka)
                    free[B] = k
                    tm = dve.tt(MX[:, ch, :], e[:, 0:256], e[:, 256:512], ADD, k)
                for s_ in (slot, slot2, slot3):
                    rel[s_] = t
            for h in range(2):
                (wt,), tw, slot = slab((A["w_o_2"][l][:, h * 512:h * 512 + 512].rearrange("(c p) n -> p c n", p=P),
                                        0, 8, 512))
                for b in range(2):
                    B = 2 * h + b
                    pe.wait(free[B], tw, tm)
                    for c in range(8):
                        t = pe.mm(PS[:, B, :], MX[:, c, b * P:b * P + P], wt[:, c, :], c == 0, c == 7, last=(c == 7))
                    xh = X[:, b, h * 512:h * 512 + 512]
                    T = M2[:, 0:512]
                    free[B] = k = dve.tt(T, PS[:, B, :], GB[:, h * 512:h * 512 + 512], MUL, t, tgb, *xtok)
                    xtok[b] = dve.tt(xh, xh, T, ADD, k)
                rel[slot] = t

        mix_first(0)
        ffn_first()
        mix_first(1)
        moe()
        for l in range(2):
            ffn_second(l, 0)
            mix_second(l)
            ffn_second(l, 1)
        s_f, s_out = sem("s_f"), sem("s_out")
        sp.do(lambda e: e.dma_start(GB[:, :], A["final_g_2"].partition_broadcast(P)).then_inc(s_f, 16), *xtok)
        for b in range(2):
            t = sca.act(XS[:, b, :], X[:, b, :], ACT.Square, *xtok, acc=SM[:, b:b + 1])
            t = dve.ts(SM[:, 2 + b:3 + b], SM[:, b:b + 1], 1.0 / D, EPS, MUL, ADD, t)
            t = dve.rsqrt(SM[:, 4 + b:5 + b], SM[:, 2 + b:3 + b], SM[:, 6 + b:7 + b], t)
            t = dve.stt(XS[:, b, :], X[:, b, :], SM[:, 4 + b:5 + b], GB[:, :], MUL, MUL, t, (s_f, 16))
            o = out[0].rearrange("(b p) n -> b p n", p=P)[b]
            sp.do(lambda e, o=o, b=b: e.dma_start(o, XS[:, b, :]).then_inc(s_out, 16), t)
        sp.wait((s_out, 32))

        block = ctx.enter_context(nc.Block())

        @block.sync
        def _(e):
            sp.run(e)

        @block.gpsimd
        def _(e):
            pool.run(e)

        @block.scalar
        def _(e):
            sca.run(e)

        @block.vector
        def _(e):
            dve.run(e)

        @block.tensor
        def _(e):
            pe.run(e)


_INS = ['x', 'positions', 'attn_norm_g', 'ffn_norm_g', 'w_in', 'w_out', 'q_norm_g', 'k_norm_g', 'cmp_pos_k',
        'cmp_w1_k', 'cmp_w2_k', 'cmp_pos_v', 'cmp_w1_v', 'cmp_w2_v', 'conv_w', 'conv_b', 'conv_ln_g', 'conv_ln_b',
        'ffn_w_gate', 'ffn_w_up', 'ffn_w_down', 'moe_router', 'moe_w_gate', 'moe_w_up', 'moe_w_down', 'c_2',
        'ada_w_2', 'ada_b_2', 'norm_g_2', 'ffn_wg_2', 'ffn_wu_2', 'ffn_wd_2', 'w_in_2', 'qk_g_2', 'lam_p_2',
        'subln_g_2', 'w_ba_2', 'w_bb_2', 'w_gate_2', 'b_gate_2', 'w_o_2', 'final_g_2']


def kernel(**inputs):
    import numpy as _np
    import concourse.bacc as _bacc
    from concourse import mybir as _mybir
    from concourse.bass_utils import run_bass_kernel_spmd as _run

    nc = _bacc.Bacc("TRN2", target_bir_lowering=False, num_devices=1)
    arrays, args = {}, {}
    for name in _INS:
        a = _np.ascontiguousarray(inputs[name])
        arrays[f"in_{name}_dram"] = a
        args[name] = nc.dram_tensor(f"in_{name}_dram", a.shape, _mybir.dt.from_np(a.dtype), kind="ExternalInput").ap()
    c = constants()
    arrays["in_cst_dram"] = c
    args["cst"] = nc.dram_tensor("in_cst_dram", c.shape, _mybir.dt.float32, kind="ExternalInput").ap()
    o = nc.dram_tensor("out_0_dram", (1, S, D), _mybir.dt.float32, kind="ExternalOutput").ap()
    build(nc, args, o)
    r = _run(nc, [arrays], core_ids=[0])
    return r.results[0]["out_0_dram"]
```

```python
from contextlib import ExitStack

import numpy as np
import concourse.bass as bass
from concourse import mybir

ALU = mybir.AluOpType
ACT = mybir.ActivationFunctionType
F32 = mybir.dt.float32
I32 = mybir.dt.int32
U32 = mybir.dt.uint32
AX = mybir.AxisListType.X
MUL, ADD, SUB, MAX, MIN = ALU.mult, ALU.add, ALU.subtract, ALU.max, ALU.min

P = 128
D = 1024
S = 256
NS = 4
EPS = 1e-6
NEG = -1e30
NE = 8
F1 = 3584
F2 = 2816
NCMP = 15
TWO_PI = 6.283185307179586
MAGIC = 12582912.0

CI, CO, CC, CM, CV, CF, CD, CA, CT, CR = np.cumsum([0, 128, 128, 128, 30, 2, 8, 512, 128, 128]).tolist()
NCONST = CR + 256
CAP = 128


def constants():
    c = np.zeros((P, NCONST), np.float32)
    p = np.arange(P)
    c[:, CI:CI + 128] = np.eye(P)
    c[:, CO:CO + 128] = 1.0
    c[:, CC:CC + 128] = np.where(p[None, :] <= p[:, None], 0.0, NEG)
    ends = np.arange(NCMP) * 16 + 31
    for b in range(2):
        t = b * P + p
        ok = ends[None, :] <= t[:, None]
        c[:, CM + b * 15:CM + b * 15 + 15] = np.where(ok, 0.0, NEG)
        c[:, CV + b] = ok.any(1)
        c[:, CD + b * 256:CD + b * 256 + 256] = np.abs(t[:, None] - np.arange(256)[None, :])
        inv = 1.0 / (np.float32(10000.0) ** (np.arange(0, 32, 2, dtype=np.float32) / 32))
        row = (t // 64 - 2).astype(np.float32)
        col = (t % 64 - 32).astype(np.float32)
        ang = np.stack([row[:, None] * inv, col[:, None] * inv], 1)
        c[:, CA + b * 64:CA + b * 64 + 32] = np.cos(ang).reshape(P, 32)
        c[:, CA + b * 64 + 32:CA + b * 64 + 64] = np.sin(ang).reshape(P, 32)
    c[:, CF:CF + 8] = (500000.0 ** (-2.0 * np.arange(8) / 16)).astype(np.float32)[None]
    c[:, CT:CT + 128] = p[:, None] < p[None, :]
    c[:, CR:CR + 128] = np.where(p < CAP, p, -1)[None, :]
    c[:, CR + 128:CR + 256] = p[None, :] + CAP
    return c


class Queue:

    def __init__(self, sem):
        self.sem, self.n, self.q, self.seen = sem, 0, [], {}

    def wait(self, *toks):
        for t in toks:
            if t is not None and self.seen.get(t[0].name, 0) < t[1]:
                self.seen[t[0].name] = t[1]
                self.q.append(lambda e, t=t: e.wait_ge(t[0], t[1]))

    def do(self, f, *w):
        self.wait(*w)
        self.q.append(f)

    def inc(self, f, *w):
        self.wait(*w)
        self.n += 1
        self.q.append(lambda e: f(e).then_inc(self.sem, 1))
        return (self.sem, self.n)

    def run(self, e):
        for f in self.q:
            f(e)


class PE(Queue):
    def mm(self, out, lhsT, rhs, start, stop, *w, last=False):
        def f(e):
            return e.matmul(out, lhsT, rhs, start=start, stop=stop)
        if last:
            return self.inc(f, *w)
        self.do(f, *w)

    def tr(self, out, in_, ident, *w, last=False):
        def f(e):
            return e.transpose(out, in_, ident)
        if last:
            return self.inc(f, *w)
        self.do(f, *w)


class DVE(Queue):
    def tt(self, out, a, b, op, *w):
        return self.inc(lambda e: e.tensor_tensor(out, a, b, op), *w)

    def ts(self, out, a, s1, s2, op0, op1, *w):
        if s2 is None:
            return self.inc(lambda e: e.tensor_scalar(out, a, s1, None, op0), *w)
        return self.inc(lambda e: e.tensor_scalar(out, a, s1, s2, op0, op1), *w)

    def stt(self, out, a, s, b, op0, op1, *w):
        return self.inc(lambda e: e.scalar_tensor_tensor(out=out, in0=a, scalar=s, in1=b, op0=op0, op1=op1), *w)

    def rcp(self, out, a, *w):
        return self.inc(lambda e: e.reciprocal(out, a), *w)

    def rsqrt(self, y, x, a, *w):
        t = self.ts(y.bitcast(I32), x.bitcast(I32), -0.5, 1597463007.0, MUL, ADD, *w)
        t = self.ts(x, x, -0.5, None, MUL, None, t)
        for _ in range(3):
            t = self.tt(a, y, y, MUL, t)
            t = self.tt(a, a, x, MUL, t)
            t = self.stt(y, a, 1.5, y, ADD, MUL, t)
        return t

    def red(self, out, a, op, *w, neg=False):
        return self.inc(lambda e: e.tensor_reduce(out, a, AX, op, negate=neg), *w)

    def cp(self, out, a, *w):
        return self.inc(lambda e: e.tensor_copy(out, a), *w)

    def ms(self, out, v, *w):
        return self.inc(lambda e: e.memset(out, v), *w)


class SCA(Queue):
    def act(self, out, a, func, *w, bias=0.0, scale=1.0, acc=None):
        if acc is None:
            return self.inc(lambda e: e.activation(out, a, func, bias=bias, scale=scale), *w)
        return self.inc(lambda e: e.activation(out, a, func, bias=bias, scale=scale, accum_out=acc), *w)

    def cp(self, out, a, *w):
        return self.inc(lambda e: e.activation(out, a, ACT.Copy), *w)


def bc(ap, shape, at):
    for i in at:
        ap = ap.unsqueeze(i)
    return ap.to_broadcast(shape)


def build(nc, A, out):
    with ExitStack() as ctx:
        def sb(name, shape, dt=F32):
            return ctx.enter_context(nc.sbuf_tensor(name, shape, dt))

        def sem(name):
            return ctx.enter_context(nc.semaphore(name))

        pe, dve, sca, pool, sp = PE(sem("s_pe")), DVE(sem("s_dve")), SCA(sem("s_act")), DVE(sem("s_pool")), Queue(sem("s_sp"))
        PS = ctx.enter_context(nc.psum_tensor("PS", [P, 8, 512], F32))
        free = [None] * 8

        ring = sb("ring", [P, NS, 4096])
        GS = sb("GS", [P, 8, 512])
        s_ring = [sem(f"s_ring{i}") for i in range(NS)]
        C = sb("C", [P, NCONST])
        X = sb("X", [P, 2, D])
        XT = sb("XT", [P, 8, S])
        R = sb("R", [P, 4608 + 4096])
        PR = R[:, 0:4608]
        HT = R[:, 0:7168].rearrange("p (c n) -> p c n", c=28)
        PB = R[:, 4608:4608 + 2048].rearrange("p (g n) -> p g n", g=2)
        PTB = R[:, 4608 + 2048:4608 + 4096].rearrange("p (g n) -> p g n", g=2)
        TMP = R[:, 4608:4608 + 4096]
        XS = (R[:, 7168:8192], R[:, 4608:5632])
        QT = sb("QT", [P, 8, S])
        EH = QT[:, :, :].rearrange("p a n -> p (a n)").rearrange("p (k i n) -> p k i n", k=2, i=2)
        KZ = sb("KZ", [P, 3072])
        MT = sb("MT", [P, 8, S])
        OA = sb("OA", [P, 2, 512])
        M2 = sb("M2", [P, 3096])
        GB = sb("GB", [P, D])
        ACC = sb("ACC", [P, 2, 512])
        VR = MT[:, 0:2, :].rearrange("p a (b n) -> p (a b) n", n=P)[:, 0:3, :]
        ADB = MT[0:72, 2, 0:P]
        VC = sb("VC", [P, 3, P])
        CWR = OA[0:31, :, :]
        CW = sb("CW", [P, 8, 31])
        W2 = sb("W2", [P, 4, 64])
        RT = sb("RT", [P, 8, 8])
        QKG = sb("QKG", [P, 2, 4, 64])
        QG2 = sb("QG2", [P, 2, 2, 64])
        LP = sb("LP", [P, 2, 256])
        SG = sb("SG", [P, 2, P])
        CACT = sb("CACT", [P, 2, 8])
        MODC = sb("MODC", [P, 2, 72])
        POSI = sb("POSI", [P, 3], I32)
        POSF = sb("POSF", [P, 3])
        CS = sb("CS", [P, 2, 3, 8])
        AN = sb("AN", [P, 4, 24])
        SM = sb("SM", [P, 512])
        MOSTI = sb("MOSTI", [P, 1], I32)

        ident = C[:, CI:CI + 128]
        ones = C[:, CO:CO + 128]

        cnt = [0] * NS
        rel = [None] * NS
        turn = [0]

        def slab(*parts):
            i = turn[0] % NS
            turn[0] += 1
            sp.wait(rel[i])
            views = []
            for src, at, c, w in parts:
                dst = ring[:, i, at:at + c * w].rearrange("p (c n) -> p c n", c=c)
                cnt[i] += 16
                sp.do(lambda e, dst=dst, src=src: e.dma_start(dst, src).then_inc(s_ring[i], 16))
                views.append(dst)
            return views, (s_ring[i], cnt[i]), i

        s_c, s_x, s_s = sem("s_c"), sem("s_x"), sem("s_s")
        sp.do(lambda e: e.dma_start(X[:, :, :], A["x"][0].rearrange("(b p) n -> p b n", p=P)).then_inc(s_x, 16))
        sp.do(lambda e: e.dma_start(C[:, :], A["cst"]).then_inc(s_c, 16))
        tc, tx = (s_c, 16), (s_x, 16)
        t0 = pool.ms(VR[:, :, :], 0.0)
        t1 = pool.ms(POSI[:, :], 0)
        ns = [0]

        s_v = sem("s_v")
        nv = [0]

        def first(dst, src):
            nv[0] += 16
            sca.do(lambda e: e.dma_start(dst, src).then_inc(s_v, 16), t0, t1)

        def small(dst, src, odd=False):
            ns[0] += 16
            pool.do(lambda e: e.dma_start(dst, src, allow_slow_non_contiguous=odd).then_inc(s_s, 16), t1)

        def rows(name):
            a = A[name]
            if len(a.shape) == 1:
                return a.rearrange("(r n) -> r n", n=P)
            if len(a.shape) == 2:
                return a.rearrange("l (r n) -> (l r) n", n=P)
            return a.rearrange("l k (r n) -> (l k r) n", n=P)

        VAT = {}
        for tile, names in enumerate((("attn_norm_g", "ffn_norm_g", "norm_g_2", "b_gate_2"),
                                      ("conv_b", "conv_ln_g", "conv_ln_b"), ())):
            r = 0
            for nm in names:
                a = rows(nm)
                n = a.shape[0]
                first(VR[r:r + n, tile, :], a)
                VAT[nm] = (tile, r)
                r += n
        for l in range(2):
            for j, nm in enumerate(("cmp_pos_k", "cmp_pos_v")):
                r = 24 + 32 * l + 16 * j
                first(VR[r:r + 16, 1, :], A[nm][l].rearrange("(r t) d -> r (t d)", t=2))
                VAT[nm, l] = (1, r)
        first(VR[0:72, 2, :], A["ada_b_2"][0].rearrange("(r n) -> r n", n=P))
        first(ADB, A["ada_b_2"][1].rearrange("(r n) -> r n", n=P))
        first(CWR[:, :, :], A["conv_w"].rearrange("l k n -> k l n"))
        tvr = (s_v, nv[0])
        for l in range(2):
            for j, nm in enumerate(("cmp_w2_k", "cmp_w2_v")):
                small(W2[:, 2 * l + j, :], A[nm][l])
        small(RT[:, :, :], A["moe_router"][0].rearrange("(c p) e -> p c e", p=P))
        small(QKG[:, :, 0, :], A["q_norm_g"].partition_broadcast(P))
        small(QKG[:, :, 1:4, :], A["k_norm_g"].partition_broadcast(P))
        G12 = sb("G12", [P, 12, 64])
        small(QG2[:, :, :, :], A["qk_g_2"].partition_broadcast(P))
        small(LP[:, :, :], A["lam_p_2"].rearrange("l a d -> l (a d)").partition_broadcast(P))
        small(SG[:, :, :], A["subln_g_2"].partition_broadcast(P))
        small(CACT[:, 0, :], A["c_2"][0].rearrange("(p c) -> p c", c=8))
        for b in range(2):
            small(POSI[:, b:b + 1], A["positions"][0, b * P:b * P + P].rearrange("(p a) -> p a", a=1))
        small(POSI[0:NCMP, 2:3], A["positions"][0, 16:256].rearrange("(n a) -> n a", a=16)[:, 15:16], odd=True)
        tsm = (s_s, ns[0])

        pe.wait(tc, tvr)
        for i in range(3):
            t = pe.tr(PS[:, i, 0:P], VR[:, i, :], ident, last=True)
            free[i] = dve.cp(VC[:, i, :], PS[:, i, 0:P], t)
        t = pe.tr(PS[:, 3, 0:72], ADB, ident[0:72, 0:72], last=True)
        ADC = sb("ADC", [P, 72])
        free[3] = dve.cp(ADC[:, :], PS[:, 3, 0:72], t)
        for j in range(8):
            t = pe.tr(PS[:, 4, 32 * j:32 * j + 31], CWR[:, j // 4, (j % 4) * P:(j % 4) * P + P], ident[0:31, 0:31],
                      last=(j == 7))
        tvc = free[4] = dve.cp(CW[:, :, :], PS[:, 4, 0:256].rearrange("p (j k) -> p j k", k=32)[:, :, 0:31], t)

        def vcol(nm, l, c, per=8):
            tile, r = VAT[nm]
            return VC[:, tile, r + l * per + c:r + l * per + c + 1]

        ada_tok = [None, None]
        ada_free = [None, None]

        def ada_steps():
            for l in range(2):
                for s in range(18):
                    (w,), tw, slot = slab((A["ada_w_2"][l][:, s * 512:s * 512 + 512].rearrange("(p c) n -> p c n", c=8),
                                           0, 8, 512))
                    a = ACC[:, s % 2, :]
                    t = dve.ts(a, w[:, 0, :], CACT[:, 1, 0:1], None, MUL, None, tw, tcact[0], ada_free[s % 2])
                    for c in range(1, 8):
                        t = dve.stt(a, w[:, c, :], CACT[:, 1, c:c + 1], a, MUL, ADD, t)
                    rel[slot] = t
                    yield
                    pe.wait(t, free[7])
                    for c in range(4):
                        t = pe.mm(PS[:, 7, c:c + 1], a[:, c * P:c * P + P], ones[:, 0:1], True, True, last=(c == 3))
                    ada_free[s % 2] = t
                    ab = VC[:, 2, 4 * s:4 * s + 4] if l == 0 else ADC[:, 4 * s:4 * s + 4]
                    free[7] = ada_tok[l] = dve.tt(MODC[:, l, 4 * s:4 * s + 4], PS[:, 7, 0:4], ab, ADD, t, tvc)
                    yield

        steps = ada_steps()
        trope, tcact = [None, None], [None]

        def late_setup():
            t = dve.cp(POSF[:, :], POSI[:, :], tsm)
            an = AN[:, 0, :].rearrange("p (s j) -> p s j", j=8)
            t = dve.tt(an, bc(POSF[:, :], [P, 3, 8], (2,)), bc(C[:, CF:CF + 8], [P, 3, 8], (1,)), MUL, t, tc)
            for j, shift in ((0, 0.25), (1, 0.0)):
                k, r = AN[:, 1, :], AN[:, 2 + j, :]
                t = dve.ts(k, AN[:, 0, :], 1.0 / TWO_PI, shift, MUL, ADD, t)
                t = dve.ts(k, k, MAGIC, None, ADD, None, t)
                t = dve.ts(k, k, MAGIC, None, SUB, None, t)
                c1 = 6.28125
                c2 = float(np.float32(TWO_PI - c1).view(np.uint32) & np.uint32(0xFFFFF000))
                c2 = float(np.uint32(int(c2)).view(np.float32))
                c3 = float(np.float32(TWO_PI - c1 - c2))
                t = dve.stt(r, k, -c1, AN[:, 0, :], MUL, ADD, t)
                t = dve.stt(r, k, -c2, r, MUL, ADD, t)
                t = dve.stt(r, k, -c3, r, MUL, ADD, t)
                t = dve.ts(r, r, TWO_PI * shift, 3.1415925, ADD, MIN, t)
                t = dve.ts(r, r, -3.1415925, None, MAX, None, t)
                trope[j] = sca.act(CS[:, j, :, :].rearrange("p s j -> p (s j)"), r, ACT.Sin, t)

            t = sca.act(CACT[:, 1, :], CACT[:, 0, :], ACT.Sigmoid, tsm)
            tcact[0] = dve.tt(CACT[:, 1, :], CACT[:, 0, :], CACT[:, 1, :], MUL, t)

        def ada(n):
            for _ in range(2 * n):
                next(steps, None)

        xtok = [tx, tx]

        def norm_turn(gain, shift, *w):
            toks = [None] * 8
            for b in range(2):
                t = sca.act(XS[b], X[:, b, :], ACT.Square, xtok[b], acc=SM[:, b:b + 1])
                t = dve.ts(SM[:, 2 + b:3 + b], SM[:, b:b + 1], 1.0 / D, EPS, MUL, ADD, t)
                t = dve.rsqrt(SM[:, 4 + b:5 + b], SM[:, 2 + b:3 + b], SM[:, 6 + b:7 + b], t)
                t1 = sca.act(XS[b][:, 0:512], X[:, b, 0:512], ACT.Copy, t, scale=SM[:, 4 + b:5 + b])
                t2 = dve.ts(XS[b][:, 512:1024], X[:, b, 512:1024], SM[:, 4 + b:5 + b], None, MUL, None, t)
                pe.wait(t1, t2, tc)
                tj = []
                for j in range(4):
                    pe.wait(free[j])
                    for cc in range(2):
                        c = 2 * j + cc
                        t = pe.tr(PS[:, j, cc * 256 + b * P:cc * 256 + b * P + P], XS[b][:, c * P:c * P + P], ident,
                                  last=(cc == 1))
                    tj.append(t)
            for j in range(4):
                t = tj[j]
                for cc in range(2):
                    c = 2 * j + cc
                    src = PS[:, j, cc * 256:cc * 256 + 256]
                    if j % 2:
                        k = dve.ts(XT[:, c, :], src, gain(c), shift(c) if shift else None, MUL, ADD, t, tvc, *w)
                    elif shift:
                        k = sca.act(XT[:, c, :], src, ACT.Identity, t, tvc, *w, scale=gain(c), bias=shift(c))
                    else:
                        k = sca.act(XT[:, c, :], src, ACT.Copy, t, tvc, *w, scale=gain(c))
                    toks[c] = free[j] = k
            return toks

        def swiglu(xt, F, wg, wu, wd, finish):
            tiles = [(f, min(512, F - f)) for f in range(0, F, 512)]
            units = [(s, b) for s in range(len(tiles)) for b in range(2)]
            ht = {}
            hv = {}
            efree = [None, None]
            hfree = [None, None]
            slabs = {}

            def turn_h(i):
                s, b = units[i]
                n = tiles[s][1] // P
                B = 4 + i % 2
                h = EH[:, 1, i % 2, 0:n * P].rearrange("p (m c) -> p c m", c=n)
                pe.wait(free[B], hv[i])
                for c in range(n):
                    t = pe.tr(PS[:, B, c * P:c * P + P], h[:, c, :], ident, last=(c == n - 1))
                hfree[i % 2] = t
                ht[s, b] = free[B] = sca.cp(HT[:, 4 * s:4 * s + n, b * P:b * P + P],
                                            PS[:, B, 0:n * P].rearrange("p (c n) -> p c n", c=n), t)

            for i, (s, b) in enumerate(units):
                f, w = tiles[s]
                if b == 0:
                    slabs[s] = [slab((a[:, f:f + w].rearrange("(c p) n -> p c n", p=P), 0, 8, w)) for a in (wg, wu)]
                g, u = PS[:, 2 * (i % 2), 0:w], PS[:, 2 * (i % 2) + 1, 0:w]
                tk = []
                for o, bank, ((wt,), tw, slot) in ((g, 2 * (i % 2), slabs[s][0]), (u, 2 * (i % 2) + 1, slabs[s][1])):
                    pe.wait(free[bank], tw)
                    for c in range(8):
                        t = pe.mm(o, XT[:, c, b * P:b * P + P], wt[:, c, :], c == 0, c == 7, xt[c], last=(c == 7))
                    tk.append(t)
                    if b == 1:
                        rel[slot] = t
                e, h = EH[:, 0, i % 2, 0:w], EH[:, 1, i % 2, 0:w]
                t = sca.act(e, g, ACT.Sigmoid, tk[0], efree[i % 2])
                t = dve.tt(e, e, g, MUL, t)
                free[2 * (i % 2)] = t
                t = dve.tt(h, e, u, MUL, t, tk[1], hfree[i % 2])
                free[2 * (i % 2) + 1] = efree[i % 2] = hv[i] = t
                if i:
                    turn_h(i - 1)
                ada(1)
            turn_h(len(units) - 1)
            yb = (6, 0)
            for s, (f, w) in enumerate(tiles):
                n = w // P
                (wt,), tw, slot = slab((wd[f:f + w, :].rearrange("(p c) n -> p c n", c=n), 0, n, D))
                pe.wait(tw)
                for b in range(2):
                    pe.wait(ht[s, b])
                    if s == 0:
                        pe.wait(free[yb[b]], free[yb[b] + 1])
                    for c in range(n):
                        for h in range(2):
                            end = s == len(tiles) - 1 and c == n - 1
                            t = pe.mm(PS[:, yb[b] + h, :], HT[:, 4 * s + c, b * P:b * P + P],
                                      wt[:, c, h * 512:h * 512 + 512], s == 0 and c == 0, end,
                                      last=(c == n - 1 and h == 1))
                    if s == len(tiles) - 1:
                        free[yb[b]] = free[yb[b] + 1] = finish(b, PS[:, yb[b]:yb[b] + 2, :].rearrange("p h n -> p (h n)"), t)
                rel[slot] = t

        def project(w, n, xt, place=None):
            toks = [None, None]
            k = 0
            for f in range(0, n, 512):
                c1 = min(512, n - f)
                (wt,), tw, slot = slab((w[:, f:f + c1].rearrange("(c p) n -> p c n", p=P), 0, 8, c1))
                for b in range(2):
                    B = k % 4
                    k += 1
                    pe.wait(free[B], tw)
                    for c in range(8):
                        t = pe.mm(PS[:, B, 0:c1], XT[:, c, b * P:b * P + P], wt[:, c, :], c == 0, c == 7, xt[c],
                                  last=(c == 7))
                    if b == 1:
                        rel[slot] = t
                    for lo, hi, to in (place[f] if place else ((0, c1, f),)):
                        dst = PR[:, b * 2304 + to:b * 2304 + to + hi - lo]
                        if b == 0:
                            free[B] = toks[b] = sca.cp(dst, PS[:, B, lo:hi], t)
                        else:
                            free[B] = toks[b] = dve.cp(dst, PS[:, B, lo:hi], t)
            return toks

        PRB = PR[:, :].rearrange("p (b n) -> p b n", b=2)

        def heads(lo, n):
            return PRB[:, :, lo:lo + n * 64].rearrange("p b (h d) -> p b h d", d=64)

        def norm_heads(x, n, np_, nb, dd, sq, ss, gain, *w):
            t = dve.tt(sq, x, x, MUL, *w)
            t = dve.red(ss, sq, ADD, t)
            m = SM[0:np_, 168:168 + nb * n].rearrange("p (b h) -> p b h", b=nb)
            t = dve.ts(m, ss, 1.0 / dd, EPS, MUL, ADD, t)
            t = dve.rsqrt(ss, m, SM[0:np_, 184:184 + nb * n].rearrange("p (b h) -> p b h", b=nb), t)
            sh = [np_, nb, n, dd]
            t = dve.tt(x, x, bc(ss, sh, (3,)), MUL, t)
            for b in range(nb):
                t2 = dve.tt(x[:, b], x[:, b], bc(gain, [np_, n, dd], (1,)), MUL, t)
            return t2

        def rope8(x, n, np_, slot, a, b, *w):
            v = x[:, :, 0:16].rearrange("p h (t j) -> p h t j", t=2)
            sh = [np_, n, 2, 8]
            ta = dve.tt(a, v, bc(CS[0:np_, 0, slot, :], sh, (1, 1)), MUL, *w)
            tb = dve.tt(b, v, bc(CS[0:np_, 1, slot, :], sh, (1, 1)), MUL, *w)
            dve.tt(v[:, :, 0, :], a[:, :, 0, :], b[:, :, 1, :], SUB, ta, tb)
            return dve.tt(v[:, :, 1, :], a[:, :, 1, :], b[:, :, 0, :], ADD, ta, tb)

        kz_pair = [None]

        class Attn:

            def __init__(self):
                self.i = 0
                self.soft = []
                self.turned = []
                self.pfree = [None, None]
                self.tfree = [None, None]

            def group(self, nk, nj, scores, soft, post, values, fill=None):
                i = self.i
                self.i += 1
                s0 = 2 * (i % 2)
                pe.wait(free[s0], free[s0 + 1])
                t = scores(s0)
                g = None
                if len(self.soft) == 2:
                    g = self.soft.pop(0)
                    self.turn(g)
                tp = soft(s0, i, t, self.pfree[i % 2])
                free[s0] = free[s0 + 1] = tp
                self.end_soft()
                self.copy_value(g)
                self.soft.append([i, nk, nj, tp, post, values, None])
                if fill:
                    fill()

            def end_soft(self):
                if self.soft and self.soft[-1][4]:
                    self.soft[-1][3] = self.soft[-1][4](self.soft[-1][0], self.soft[-1][3])
                    self.soft[-1][4] = None

            def turn(self, g):
                i, nk, nj, tp, _, _, _ = g
                ts = []
                pe.wait(tp)
                kp = min(nk, P)
                for kc in range(max(1, nk // P)):
                    pe.wait(free[4 + kc])
                    for j in range(nj):
                        src = PB[:, i % 2, j * 256 + kc * P:j * 256 + kc * P + kp]
                        t = pe.tr(PS[0:kp, 4 + kc, j * P:j * P + P], src, ident, last=(j == nj - 1))
                    ts.append(t)
                self.pfree[i % 2] = t
                g[6] = ts

            def copy_value(self, g):
                if g:
                    i, nk, nj, _, _, values, ts = g
                    te = []
                    kp = min(nk, P)
                    for kc, t in enumerate(ts):
                        dst = PTB[0:kp, i % 2, kc * 512:kc * 512 + nj * P]
                        k = (dve if kc == 0 else sca).cp(dst, PS[0:kp, 4 + kc, 0:nj * P], t, self.tfree[i % 2])
                        free[4 + kc] = k
                        te.append(k)
                if self.turned:
                    h = self.turned.pop(0)
                    self.tfree[h[0] % 2] = h[1](h[0], h[2])
                if g:
                    self.turned.append((i, values, te))

            def flush(self, fills=()):
                fills = list(fills)
                self.end_soft()
                while self.soft or self.turned:
                    g = None
                    if self.soft:
                        g = self.soft.pop(0)
                        self.turn(g)
                    self.copy_value(g)
                    if fills:
                        fills.pop(0)()

        HP = M2[:, 0:1144].rearrange("p (c n) -> p c n", c=4)
        Y = M2[:, 1144:2168].rearrange("p (c n) -> p c n", c=4)
        CB = GS[:, :, :].rearrange("p a n -> p (a n)")[:, 0:960].rearrange("p (q m n) -> p q m n", q=2, m=16)
        KVT = M2[:, 2168:2680].rearrange("p (k n) -> p k n", k=2)
        HB = M2[:, 2680:2840]
        KC15 = M2[:, 2840:2968]
        VC15 = M2[:, 2968:3096]
        KZC = SM[:, 200:264]

        def mix_first(l):
            xt = norm_turn(lambda c: vcol("attn_norm_g", l, c), None)
            if l == 0:
                late_setup()
            W = A["w_in"][l]
            tz = pool.ms(KZ[:, :], 0.0, *xtok)
            tz = pool.ms(HP[:, :, 0:30], 0.0, *xtok)
            tz = pool.ms(KZC, 0.0, *xtok)
            pool.wait(tsm)
            for lo, n, gi in ((0, 8, 0), (8, 2, 2), (10, 2, 3)):
                tg12 = pool.cp(G12[:, lo:lo + n, :], bc(QKG[:, l, gi, :], [P, n, 64], (1,)))
            tp = project(W, 1304, xt, {0: ((0, 512, 0),), 512: ((0, 256, 768), (256, 384, 512), (384, 512, 1024)),
                                       1024: ((0, 128, 640), (128, 280, 1152))})

            sl = []
            glu = {}

            def up(ch):
                if not sl:
                    sl.extend(slab((W[:, f:f + 512].rearrange("(c p) n -> p c n", p=P), 0, 8, 512)) for f in (1304, 1816))
                B = ch
                pe.wait(free[B], sl[0][1], sl[1][1])
                for q in range(2):
                    for c in range(8):
                        t = pe.mm(PS[:, B, q * 256:q * 256 + 256], sl[q][0][0][:, c, ch * P:ch * P + P], XT[:, c, :],
                                  c == 0, c == 7, last=(c == 7 and q == 1))
                e = TMP[:, 3072 + 256 * ch:3072 + 256 * ch + 256]
                glu[ch] = (t, sca.act(e, PS[:, B, 256:512], ACT.Sigmoid, t), e)
                rel[sl[0][2]] = rel[sl[1][2]] = t

            thp = [None] * 4

            def glue(ch):
                t, k, e = glu[ch]
                free[ch] = thp[ch] = dve.tt(HP[:, ch, 30:286], e, PS[:, ch, 0:256], MUL, k, tz)

            gt = SM[:, 16:64].rearrange("p (b n) -> p b n", b=2)
            tg = sca.act(gt, PRB[:, :, 1280:1304], ACT.Sigmoid, *tp)
            (w1k, w1v), tw1, slot1 = slab((A["cmp_w1_k"][l].rearrange("(m p) h -> p m h", p=P), 0, 16, P),
                                          (A["cmp_w1_v"][l].rearrange("(m p) h -> p m h", p=P), 2048, 16, P))
            tkv = []
            for q in range(2):
                pe.wait(free[6 + q], *tp)
                for v in range(2):
                    for b in range(2):
                        t = pe.tr(PS[0:64, 6 + q, v * 256 + b * P:v * 256 + b * P + P],
                                  PRB[:, b, 768 + 128 * q + v * 64:832 + 128 * q + v * 64], ident,
                                  last=(v == 1 and b == 1))
                tkv.append(t)
            sq = TMP[:, 0:1536].rearrange("p (b n) -> p b n", b=2)
            for b in range(2):
                t = sca.act(sq[:, b, :], PRB[:, b, 0:768], ACT.Square, tp[b])
            up(0)
            up(1)
            ss = SM[:, 64:88]
            t = dve.red(ss, TMP[:, 0:1536].rearrange("p (h d) -> p h d", d=64), ADD, t)
            m = SM[:, 400:424]
            t = dve.ts(m, ss, 1.0 / 64, EPS, MUL, ADD, t)
            t = dve.rsqrt(ss, m, SM[:, 424:448], t)
            q12 = heads(0, 12)
            t = dve.tt(q12, q12, bc(ss.rearrange("p (b h) -> p b h", b=2), [P, 2, 12, 64], (3,)), MUL, t)
            flat = PRB[:, :, 0:768]
            t = dve.tt(flat, flat, bc(G12[:, :, :].rearrange("p h d -> p (h d)"), [P, 2, 768], (1,)), MUL, t, tg12)
            pgain = t
            tq = [None, None]
            for b in range(2):
                ra = TMP[:, 1536 + 384 * b:1728 + 384 * b].rearrange("p (h t j) -> p h t j", t=2, j=8)
                rb = TMP[:, 1728 + 384 * b:1920 + 384 * b].rearrange("p (h t j) -> p h t j", t=2, j=8)
                tq[b] = rope8(q12[:, b], 12, P, b, ra, rb, t, trope[1])
            KZ1 = KZ[:, 0:2048].rearrange("p (k v r n) -> p k v r n", k=2, v=2, r=2)
            tk = None

            def swap(dst, src, np_, *w):
                dve.cp(dst[:, 0:64], src[:, 64:128], *w)
                return dve.cp(dst[:, 64:128], src[:, 0:64], *w)

            SW = TMP[:, 2304:2816].rearrange("p (k b n) -> p k b n", k=2, b=2)
            tsw = {}
            for k in range(2):
                for b in range(2):
                    tsw[k, b] = swap(SW[:, k, b, :], PRB[:, b, 512 + 128 * k:640 + 128 * k], P, tq[b])
            tcb = []
            for q in range(2):
                src = PS[0:64, 6 + q, :].rearrange("p (n t) -> p t n", t=2)
                kt = KVT[:, q, :]
                dve.cp(kt[0:64, :], src[:, 0, :], tkv[q])
                free[6 + q] = t = dve.cp(kt[64:128, :], src[:, 1, :], tkv[q])
                ktv = kt.rearrange("p (v n) -> p v n", v=2)
                ap = ktv[:, :, 0:1]
                tile, r = VAT[("cmp_pos_k", "cmp_pos_v")[q], l]
                CBq = CB[:, q]
                for v in range(2):
                    win = ktv[:, v, 0:120].rearrange("p (n m) -> p m n", m=8)
                    win2 = ktv[:, v, 8:128].rearrange("p (n m) -> p m n", m=8)
                    for hf, wn in ((0, win), (1, win2)):
                        pos = bc(VC[:, tile, r + 8 * hf:r + 8 * hf + 8], [P, 8, 15], (2,))
                        k = dve.tt(CBq[:, 8 * hf:8 * hf + 8, 15 * v:15 * v + 15], wn, pos, ADD, t, tvc)
                tcb.append(k)
            glue(0)
            glue(1)
            for b in range(2):
                pe.wait(free[4 + b], tq[b])
                for pr in range(4):
                    t = pe.tr(PS[:, 4 + b, pr * P:pr * P + P], PRB[:, b, pr * P:pr * P + P], ident, last=(pr == 3))
                free[4 + b] = tqt = sca.cp(QT[:, 0:4, b * P:b * P + P],
                                           PS[:, 4 + b, :].rearrange("p (c n) -> p c n", c=4), t)
            for k in range(2):
                B = 6 + k
                pe.wait(free[B])
                for b in range(2):
                    pe.tr(PS[:, B, b * P:b * P + P], PRB[:, b, 512 + 128 * k:640 + 128 * k], ident, tsw[k, b])
                    t = pe.tr(PS[:, B, 256 + b * P:256 + b * P + P], SW[:, k, b, :], ident, last=(b == 1))
                sca.cp(KZ1[0:64, k, 0, 0, :], PS[0:64, B, 0:256], t, tz)
                sca.cp(KZ1[64:128, k, 1, 1, :], PS[64:128, B, 0:256], t)
                sca.cp(KZ1[0:64, k, 1, 0, :], PS[0:64, B, 256:512], t)
                free[B] = tk = sca.cp(KZ1[64:128, k, 0, 1, :], PS[64:128, B, 256:512], t)
            up(2)
            pe.wait(*tcb, tw1, free[4], free[5])
            thid = []
            for q, w1 in ((0, w1k), (1, w1v)):
                for mm_ in range(16):
                    t = pe.mm(PS[:, 4, 32 * q:32 * q + 30], w1[:, mm_, :], CB[:, q, mm_, :], mm_ == 0, mm_ == 15,
                              last=(mm_ == 15))
            rel[slot1] = t
            x, u = HB[:, 0:62], HB[:, 62:124]
            t = dve.ms(HB[:, 0:124], 0.0, t)
            for q in range(2):
                t = dve.cp(x[:, 32 * q:32 * q + 30], PS[:, 4, 32 * q:32 * q + 30], t)
            free[4] = t
            t = dve.tt(u, x, x, MUL, t)
            t = dve.ts(u, u, 0.044715, 1.0, MUL, ADD, t)
            t = dve.tt(u, u, x, MUL, t)
            t = sca.act(u, u, ACT.Sigmoid, t, scale=2.0 * 0.7978845608028654)
            t = dve.tt(u, x, u, MUL, t)
            up(3)
            pe.wait(t, free[5])
            for q in range(2):
                for v in range(2):
                    t = pe.mm(PS[0:NCMP, 5, 128 * q + v * 64:128 * q + v * 64 + 64],
                              u[:, 32 * q + v * 15:32 * q + v * 15 + 15], W2[:, 2 * l + q, :], True, True,
                              last=(v == 1 and q == 1))
            dve.cp(KC15[0:NCMP, :], PS[0:NCMP, 5, 0:128], t)
            free[5] = tcv = dve.cp(VC15[0:NCMP, :], PS[0:NCMP, 5, 128:256], t)
            glue(2)
            glue(3)
            xk = KC15[0:NCMP, :].rearrange("p (b h d) -> p b h d", b=1, d=64)
            sqk = HB[0:NCMP, 0:128].rearrange("p (b h d) -> p b h d", b=1, d=64)
            t = norm_heads(xk, 2, NCMP, 1, 64, sqk, SM[0:NCMP, 100:102].rearrange("p (b h) -> p b h", b=1),
                           QKG[0:NCMP, l, 1, :], tcv)
            ra = SM[0:NCMP, 104:136].rearrange("p (h t j) -> p h t j", t=2, j=8)
            rb = SM[0:NCMP, 136:168].rearrange("p (h t j) -> p h t j", t=2, j=8)
            tkc = rope8(xk[:, 0], 2, NCMP, 2, ra, rb, t, trope[1])
            sw = HB[0:NCMP, 0:128]
            tswc = swap(sw, KC15[0:NCMP, :], NCMP, tkc)
            KC = KZC.rearrange("p (v r n) -> p v r n", v=2, r=2)

            def turn_kc():
                pe.wait(tswc, free[5])
                pe.tr(PS[:, 5, 0:NCMP], KC15[0:NCMP, :], ident[0:NCMP, 0:NCMP])
                t = pe.tr(PS[:, 5, 16:16 + NCMP], sw, ident[0:NCMP, 0:NCMP], last=True)
                dve.cp(KC[0:64, 0, 0, 0:15], PS[0:64, 5, 0:15], t, tz)
                dve.cp(KC[64:128, 1, 1, 0:15], PS[64:128, 5, 0:15], t)
                dve.cp(KC[0:64, 1, 0, 0:15], PS[0:64, 5, 16:31], t)
                free[5] = tkcc[0] = dve.cp(KC[64:128, 0, 1, 0:15], PS[64:128, 5, 16:31], t)

            tkcc = [None]
            turn_kc()

            CT = GS[:, 2:6, :].rearrange("p a (b n) -> p (a b) n", b=2)
            prod = [None] * 8
            add = [None] * 8
            yp = {}

            def conv_pair():
                m = 0
                for k in range(31):
                    for ch in (3, 2):
                        h, w = HP[:, ch, k:k + 256], CW[:, 4 * l + ch, k:k + 1]
                        if k == 0:
                            yp[ch] = sca.act(Y[:, ch, :], h, ACT.Identity, thp[ch], tvc, scale=w,
                                             bias=vcol("conv_b", l, ch, 4))
                        else:
                            i = m % 8
                            m += 1
                            t = sca.act(CT[:, i, :], h, ACT.Copy, add[i], *tcb, scale=w)
                            yp[ch] = add[i] = pool.tt(Y[:, ch, :], Y[:, ch, :], CT[:, i, :], ADD, t, yp[ch])
                        yield True

            def conv_own():
                for k in range(31):
                    for ch in range(2):
                        h, w = HP[:, ch, k:k + 256], CW[:, 4 * l + ch, k:k + 1]
                        if k == 0:
                            yp[ch] = dve.ts(Y[:, ch, :], h, w, vcol("conv_b", l, ch, 4), MUL, ADD, thp[ch], tvc)
                        else:
                            yp[ch] = dve.stt(Y[:, ch, :], h, w, Y[:, ch, :], MUL, ADD, yp[ch])
                        yield True
            cva, cvb = conv_own(), conv_pair()

            def taps():
                for _ in range(7):
                    next(cva, None)
                    next(cvb, None)

            LN = GS[:, :, :].rearrange("p a n -> p (a n)")
            SQ = LN[:, 1024:2048].rearrange("p (c n) -> p c n", c=4)
            mean, rs, rs2, rs3 = (LN[:, 2048 + 256 * i:2304 + 256 * i] for i in range(4))
            ln = {}

            def ln_mean(B):
                pe.wait(free[B], *[yp[ch] for ch in range(4)])
                for ch in range(4):
                    t = pe.mm(PS[:, B, 0:256], ones, Y[:, ch, :], ch == 0, ch == 3, last=(ch == 3))
                free[B] = t = sca.act(mean, PS[:, B, 0:256], ACT.Copy, t, scale=1.0 / 512)
                ln[0] = dve.tt(Y[:, :, :], Y[:, :, :], bc(mean, [P, 4, 256], (1,)), SUB, t)
                ln[1] = sca.act(SQ, Y[:, :, :], ACT.Square, ln[0])

            def ln_var(B):
                pe.wait(ln[1], free[B])
                for ch in range(4):
                    t = pe.mm(PS[:, B, 0:256], ones, SQ[:, ch, :], ch == 0, ch == 3, last=(ch == 3))
                free[B] = t = dve.ts(rs, PS[:, B, 0:256], 1.0 / 512, EPS, MUL, ADD, t)
                t = dve.rsqrt(rs2, rs, rs3, t)
                ln[2] = dve.tt(Y[:, :, :], Y[:, :, :], bc(rs2, [P, 4, 256], (1,)), MUL, t)

            def ln_silu():
                g, b_ = [[vcol(nm, l, ch, 4) for ch in range(4)] for nm in ("conv_ln_g", "conv_ln_b")]
                ks = []
                for ch in range(4):
                    ks.append(sca.act(SQ[:, ch, :], Y[:, ch, :], ACT.Sigmoid, ln[2], scale=g[ch], bias=b_[ch]))
                for ch in range(4):
                    k = dve.ts(Y[:, ch, :], Y[:, ch, :], g[ch], b_[ch], MUL, ADD, ks[ch])
                ln[3] = dve.tt(MT[:, 4:8, :], Y[:, :, :], SQ, MUL, k)

            at = Attn()
            oa = [None, None]
            gv = gt.rearrange("p b (h r) -> p b r h", r=3)
            nob = [0]
            order = (1, 2, 0)

            def one(b, kind, v, fill=None):
                nk = NCMP if kind == 0 else P * (b + 1)
                so = 264 + 16 * (b * 3 + kind)
                mx, sm = SM[:, so + 4 * v:so + 4 * v + 4], SM[:, so + 8 + 4 * v:so + 12 + 4 * v]

                def scores(s0):
                    pe.wait(tqt, tk, tkcc[0])
                    for j in range(4):
                        h = 4 * v + j
                        rhs = KC[:, v, j % 2, 0:15] if kind == 0 else KZ1[:, kind - 1, v, j % 2, 0:nk]
                        t = pe.mm(PS[:, s0 + j // 2, (j % 2) * 256:(j % 2) * 256 + nk],
                                  QT[:, h // 2, b * P:b * P + P], rhs, True, True, last=(j == 3))
                    return t

                def soft(s0, i, t, pf):
                    s4 = PS[:, s0:s0 + 2, :].rearrange("p k (j n) -> p (k j) n", j=2)
                    if kind == 0:
                        dg, mk = s4[:, :, 0:15], C[:, CM + 15 * b:CM + 15 * b + 15]
                    else:
                        dg, mk = s4[:, :, nk - P:nk], C[:, CC:CC + P]
                    t = dve.tt(dg, dg, bc(mk, [P, 4, min(nk, P)], (1,)), ADD, t)
                    t = dve.red(mx, s4[:, :, 0:nk], MAX, t, neg=True)
                    t = dve.ts(mx, mx, 0.125, None, MUL, None, t)
                    for j in range(4):
                        te = sca.act(PB[:, i % 2, j * 256:j * 256 + nk], s4[:, j, 0:nk], ACT.Exp, t, pf,
                                     bias=mx[:, j:j + 1], scale=0.125, acc=sm[:, j:j + 1])
                    return te

                def values(i, te):
                    if v == 0:
                        nob[0] += 1
                    B = 6 + nob[0] % 2
                    pe.wait(*te)
                    if v == 0:
                        pe.wait(free[B])
                    kp = min(nk, P)
                    nkc = max(1, nk // P)
                    for j in range(4):
                        h = 4 * v + j
                        for kc in range(nkc):
                            if kind == 0:
                                vv = VC15[0:NCMP, v * 64:v * 64 + 64]
                            else:
                                vv = PRB[:, kc, 896 + 128 * kind + v * 64:960 + 128 * kind + v * 64]
                            t = pe.mm(PS[:, B, h * 64:h * 64 + 64], PTB[0:kp, i % 2, kc * 512 + j * P:kc * 512 + j * P + P],
                                      vv, kc == 0, kc == nkc - 1, last=(j == 3 and kc == nkc - 1))
                    if v == 1:
                        cf = SM[:, so + 8:so + 16]
                        k = dve.rcp(cf, cf, *te)
                        k = dve.tt(cf, cf, gv[:, b, kind, :], MUL, k, tg)
                        if kind == 0:
                            k = dve.ts(cf, cf, C[:, CV + b:CV + b + 1], None, MUL, None, k)
                        o3 = PS[:, B, :].rearrange("p (h d) -> p h d", d=64)
                        if kind == order[0]:
                            oa[b] = free[B] = dve.tt(OA[:, b, :].rearrange("p (h d) -> p h d", d=64), o3,
                                                     bc(cf, [P, 8, 64], (2,)), MUL, t, k)
                        else:
                            free[B] = k = dve.tt(TMPO.rearrange("p (h d) -> p h d", d=64), o3,
                                                 bc(cf, [P, 8, 64], (2,)), MUL, t, k)
                            oa[b] = dve.tt(OA[:, b, :], OA[:, b, :], TMPO, ADD, k, oa[b])
                    return t

                at.group(nk, 4, scores, soft, None, values, fill)

            TMPO = GB[:, 0:512]
            fills = [taps] * 9 + [lambda: ln_mean(7 - nob[0] % 2), lambda: ln_var(7 - nob[0] % 2), ln_silu]
            for kind in order:
                for b in range(2):
                    for v in range(2):
                        one(b, kind, v, fills.pop(0))
            at.flush()
            tconv = ln[3]
            for b in range(2):
                B = 2 + b
                pe.wait(free[B], oa[b])
                for c in range(4):
                    t = pe.tr(PS[:, B, c * P:c * P + P], OA[:, b, c * P:c * P + P], ident, last=(c == 3))
                free[B] = toa = sca.cp(MT[:, 0:4, b * P:b * P + P], PS[:, B, :].rearrange("p (c n) -> p c n", c=4), t)
            wo = [slab((A["w_out"][l][:, h * 512:h * 512 + 512].rearrange("(c p) n -> p c n", p=P), 0, 8, 512))
                  for h in range(2)]
            for b in range(2):
                for h, ((wt,), tw, slot) in enumerate(wo):
                    B = 4 + 2 * h + b
                    pe.wait(free[B], tw, tconv, toa)
                    for c in range(8):
                        t = pe.mm(PS[:, B, :], MT[:, c, b * P:b * P + P], wt[:, c, :], c == 0, c == 7, last=(c == 7))
                    xh = X[:, b, h * 512:h * 512 + 512]
                    free[B] = xtok[b] = dve.tt(xh, xh, PS[:, B, :], ADD, t)
                    rel[slot] = t

        def ffn_first():
            xt = norm_turn(lambda c: vcol("ffn_norm_g", 0, c), None)
            next(steps)

            def finish(b, y, t):
                xtok[b] = dve.tt(X[:, b, :], X[:, b, :], y, ADD, t)
                return xtok[b]
            swiglu(xt, F1, A["ffn_w_gate"][0], A["ffn_w_up"][0], A["ffn_w_down"][0], finish)

        def moe():
            xt = norm_turn(lambda c: vcol("ffn_norm_g", 1, c), None)
            tile, r = VAT["ffn_norm_g"]
            gain = VC[:, tile, r + 8:r + 16]
            GW = SM[:, 16:32].rearrange("p (b e) -> p b e", b=2)
            M = SM[:, 80:96].rearrange("p (b e) -> p b e", b=2)
            RK = SM[:, 96:112].rearrange("p (b e) -> p b e", b=2)
            t = None
            for b in range(2):
                pe.wait(free[b])
                for c in range(8):
                    t = pe.mm(PS[:, b, 0:8], XT[:, c, b * P:b * P + P], RT[:, c, :], c == 0, c == 7, xt[c],
                              last=(c == 7))
                lg, m8, gg = SM[:, 32:40], SM[:, 40:48], SM[:, 48:52]
                ix, fx, oh = SM[:, 56:64].bitcast(U32), SM[:, 64:72], SM[:, 72:80]
                free[b] = t = dve.cp(lg, PS[:, b, 0:8], t)
                t = dve.inc(lambda e: e.max(m8, lg), t)
                t = dve.inc(lambda e: e.max_index(ix, m8, lg), t)
                t = dve.cp(fx, ix, t)
                t = dve.tt(gg[:, 0:1], m8[:, 1:2], m8[:, 0:1], SUB, t)
                sca.act(gg[:, 2:3], gg[:, 0:1], ACT.Sigmoid, t, scale=-1.0)
                t = sca.act(gg[:, 3:4], gg[:, 0:1], ACT.Sigmoid, t)
                io = C[:, CR:CR + 8]
                t = dve.ts(GW[:, b, :], io, fx[:, 0:1], gg[:, 2:3], ALU.is_equal, MUL, t)
                t = dve.ts(oh, io, fx[:, 1:2], gg[:, 3:4], ALU.is_equal, MUL, t)
                t = dve.tt(GW[:, b, :], GW[:, b, :], oh, ADD, t)
                t = dve.ts(M[:, b, :], io, fx[:, 0:1], None, ALU.is_equal, None, t)
                t = dve.ts(oh, io, fx[:, 1:2], None, ALU.is_equal, None, t)
                t = dve.tt(M[:, b, :], M[:, b, :], oh, ADD, t)
            pe.wait(t, free[2], free[3])
            pe.mm(PS[:, 2, 0:8], C[:, CT:CT + P], M[:, 0, :], True, True)
            pe.mm(PS[:, 2, 8:16], C[:, CT:CT + P], M[:, 1, :], True, False)
            t = pe.mm(PS[:, 2, 8:16], ones, M[:, 0, :], False, True, last=True)
            pe.mm(PS[:, 3, 0:8], ones, M[:, 0, :], True, False)
            t2 = pe.mm(PS[:, 3, 0:8], ones, M[:, 1, :], False, True, last=True)
            k = dve.ts(RK, M, -1000.0, 1000.0, MUL, ADD, t)
            free[2] = trk = dve.tt(RK, RK, PS[:, 2, 0:16].rearrange("p (b e) -> p b e", b=2), ADD, k)
            most = SM[:, 120:121]
            free[3] = k = dve.red(most, PS[:, 3, 0:8], MAX, t2)
            tmost = dve.cp(MOSTI[:, :], most, k)

            XE = MT[:, :, :].rearrange("p a n -> p (a n)").rearrange("p (k c n) -> p k c n", k=2, c=8)
            HM = R[:, 0:1024].rearrange("p (k n) -> p k n", k=2)
            YS = R[:, 1024:3072].rearrange("p (k n) -> p k n", k=2)
            PG = M2[:, 0:256].rearrange("p (b n) -> p b n", b=2)
            PW = M2[:, 256:512].rearrange("p (b n) -> p b n", b=2)
            PT = M2[:, 512:1024].rearrange("p (k n) -> p k n", k=2)
            g3 = bc(gain, [P, 8, P], (2,))

            def choose(d, pw, pg, io, e, *w):
                for b in range(2):
                    d.ts(pg[:, b, :], io, RK[:, b, e:e + 1], None, ALU.is_equal, None, trk, *w)
                    t = d.ts(pw[:, b, :], io, RK[:, b, e:e + 1], GW[:, b, e:e + 1], ALU.is_equal, MUL)
                return t

            txe, tpt, tys = {}, {}, {}
            pgfree = [None]

            def turn_p(e):
                B = 4 + 2 * (e % 2)
                t = choose(dve, PW, PG, C[:, CR:CR + P], e, pgfree[0])
                pe.wait(t, free[B])
                for b in range(2):
                    t = pe.tr(PS[:, B, b * P:b * P + P], PW[:, b, :], ident, last=(b == 1))
                free[B] = tpt[e] = sca.cp(PT[:, e % 2, :], PS[:, B, 0:256], t)

            def gather(e):
                B = 4 + 2 * (e % 2)
                for k in range(2):
                    pe.wait(free[B + k])
                    for c in range(4):
                        for b in range(2):
                            t = pe.mm(PS[:, B + k, c * P:c * P + P], XS[b][:, (4 * k + c) * P:(4 * k + c) * P + P],
                                      PG[:, b, :], b == 0, b == 1, last=(c == 3 and b == 1))
                    free[B + k] = txe[e, k] = dve.tt(XE[:, e % 2, 4 * k:4 * k + 4, :],
                                                     PS[:, B + k, :].rearrange("p (c n) -> p c n", c=4),
                                                     g3[:, 4 * k:4 * k + 4, :], MUL, t)
                pgfree[0] = t

            def save_y(e, t):
                B = 4 + 2 * (e % 2)
                k = sca.cp(YS[:, e % 2, :], PS[:, B:B + 2, :].rearrange("p h n -> p (h n)"), t)
                free[B] = free[B + 1] = tys[e] = k

            def scatter(e, b):
                B = 4 + 2 * (e % 2)
                pe.wait(free[B], free[B + 1], tys[e], tpt[e])
                for h in range(2):
                    t = pe.mm(PS[:, B + h, :], PT[:, e % 2, b * P:b * P + P], YS[:, e % 2, h * 512:h * 512 + 512],
                              True, True, last=(h == 1))
                xtok[b] = dve.tt(X[:, b, :], X[:, b, :], PS[:, B:B + 2, :].rearrange("p h n -> p (h n)"), ADD, t, xtok[b])
                free[B] = free[B + 1] = xtok[b]

            units = [(e, s) for e in range(NE) for s in range(7)]
            hv, ht, hfree, efree = {}, {}, [None, None], [None, None]

            def down(i):
                e, s = units[i]
                f = 512 * s
                (wt,), tw, slot = slab((A["moe_w_down"][0, e][f:f + 512, :].rearrange("(p c) n -> p c n", c=4), 0, 4, D))
                B = 4 + 2 * (e % 2)
                pe.wait(tw, ht[i])
                if s == 0:
                    pe.wait(free[B], free[B + 1])
                for c in range(4):
                    for h in range(2):
                        t = pe.mm(PS[:, B + h, :], HM[:, i % 2, c * P:c * P + P], wt[:, c, h * 512:h * 512 + 512],
                                  s == 0 and c == 0, s == 6 and c == 3, last=(c == 3 and h == 1))
                rel[slot] = t
                if s == 6:
                    save_y(e, t)

            def turn_h(i):
                B = 2 * (i % 2)
                h = EH[:, 1, i % 2, :].rearrange("p (m c) -> p c m", c=4)
                pe.wait(free[B], hv[i])
                for c in range(4):
                    t = pe.tr(PS[:, B, c * P:c * P + P], h[:, c, :], ident, last=(c == 3))
                hfree[i % 2] = t
                ht[i] = free[B] = sca.cp(HM[:, i % 2, :], PS[:, B, :], t)

            turn_p(0)
            gather(0)
            for i, (e, s) in enumerate(units):
                f = 512 * s
                tk = []
                for B, a in ((2 * (i % 2), A["moe_w_gate"]), (2 * (i % 2) + 1, A["moe_w_up"])):
                    (wt,), tw, slot = slab((a[0, e][:, f:f + 512].rearrange("(c p) n -> p c n", p=P), 0, 8, 512))
                    pe.wait(free[B], tw)
                    for c in range(8):
                        t = pe.mm(PS[:, B, :], XE[:, e % 2, c, :], wt[:, c, :], c == 0, c == 7, txe[e, c // 4],
                                  last=(c == 7))
                    rel[slot] = t
                    tk.append(t)
                g, u = PS[:, 2 * (i % 2), :], PS[:, 2 * (i % 2) + 1, :]
                ev, h = EH[:, 0, i % 2, :], EH[:, 1, i % 2, :]
                t = sca.act(ev, g, ACT.Sigmoid, tk[0], efree[i % 2])
                t = dve.tt(ev, ev, g, MUL, t)
                free[2 * (i % 2)] = t
                t = dve.tt(h, ev, u, MUL, t, tk[1], hfree[i % 2])
                free[2 * (i % 2) + 1] = efree[i % 2] = hv[i] = t
                if i >= 1:
                    turn_h(i - 1)
                if i >= 2:
                    down(i - 2)
                if e and s in (2, 3):
                    scatter(e - 1, s - 2)
                if s == 4 and e + 1 < NE:
                    turn_p(e + 1)
                if s == 5 and e + 1 < NE:
                    gather(e + 1)
                ada(1 if (s in (3, 5) if e % 2 == 0 else s in (0, 1)) else 0)
            n = len(units)
            turn_h(n - 1)
            down(n - 2)
            down(n - 1)
            scatter(NE - 1, 0)
            scatter(NE - 1, 1)

            o_pe, o_dve, o_act = PE(sem("o_pe")), DVE(sem("o_dve")), SCA(sem("o_act"))
            s_od = sem("s_od")
            nd = [0]
            for q in (o_pe, o_dve, o_act):
                q.wait(*xtok, (pe.sem, pe.n), (sca.sem, sca.n), tmost)
            W = R[:, 0:4096]
            XO = XE[:, 0]
            HO = KZ[:, 0:512]
            YO = KZ[:, 1024:2048]
            eo, ho = EH[:, 0, 0, :], EH[:, 1, 0, :]
            last = None

            def load(src, c, *w):
                nd[0] += 16
                dst = W.rearrange("p (c n) -> p c n", c=c)
                o_act.do(lambda e: e.dma_start(dst, src).then_inc(s_od, 16), *w)
                return dst, (s_od, nd[0])

            tw_free = None
            for e in range(NE):
                t = choose(o_dve, PW, PG, C[:, CR + P:CR + 2 * P], e, last)
                o_pe.wait(t)
                for b in range(2):
                    t = o_pe.tr(PS[:, 0, b * P:b * P + P], PW[:, b, :], ident, last=(b == 1))
                tpo = o_dve.cp(PT[:, 0, :], PS[:, 0, 0:256], t)
                for k in range(2):
                    for c in range(4):
                        for b in range(2):
                            t = o_pe.mm(PS[:, 1 + k, c * P:c * P + P], XS[b][:, (4 * k + c) * P:(4 * k + c) * P + P],
                                        PG[:, b, :], b == 0, b == 1, last=(c == 3 and b == 1))
                    txo = o_dve.tt(XO[:, 4 * k:4 * k + 4, :], PS[:, 1 + k, :].rearrange("p (c n) -> p c n", c=4),
                                   g3[:, 4 * k:4 * k + 4, :], MUL, t)
                for s in range(7):
                    f = 512 * s
                    for B, a in ((3, A["moe_w_gate"]), (4, A["moe_w_up"])):
                        wt, tw = load(a[0, e][:, f:f + 512].rearrange("(c p) n -> p c n", p=P), 8, tw_free)
                        o_pe.wait(tw, txo)
                        for c in range(8):
                            t = o_pe.mm(PS[:, B, :], XO[:, c, :], wt[:, c, :], c == 0, c == 7, last=(c == 7))
                        tw_free = t
                    k = o_act.act(eo, PS[:, 3, :], ACT.Sigmoid, t)
                    k = o_dve.tt(eo, eo, PS[:, 3, :], MUL, k)
                    k = o_dve.tt(ho, eo, PS[:, 4, :], MUL, k)
                    o_pe.wait(k)
                    hc = ho.rearrange("p (m c) -> p c m", c=4)
                    for c in range(4):
                        t = o_pe.tr(PS[:, 5, c * P:c * P + P], hc[:, c, :], ident, last=(c == 3))
                    k = o_dve.cp(HO, PS[:, 5, :], t)
                    wt, tw = load(A["moe_w_down"][0, e][f:f + 512, :].rearrange("(p c) n -> p c n", c=4), 4, tw_free)
                    o_pe.wait(tw, k)
                    for c in range(4):
                        for h in range(2):
                            t = o_pe.mm(PS[:, 6 + h, :], HO[:, c * P:c * P + P], wt[:, c, h * 512:h * 512 + 512],
                                        s == 0 and c == 0, s == 6 and c == 3, last=(c == 3 and h == 1))
                    tw_free = t
                k = o_dve.cp(YO, PS[:, 6:8, :].rearrange("p h n -> p (h n)"), t)
                o_pe.wait(k, tpo)
                for b in range(2):
                    for h in range(2):
                        t = o_pe.mm(PS[:, 4 * b + h, :], PT[:, 0, b * P:b * P + P], YO[:, h * 512:h * 512 + 512],
                                    True, True, last=(h == 1))
                    last = o_dve.tt(X[:, b, :], X[:, b, :], PS[:, 4 * b:4 * b + 2, :].rearrange("p h n -> p (h n)"),
                                    ADD, t, last)
                o_pe.wait(last)
            for q in (o_pe, o_dve, o_act):
                q.wait(last, (o_act.sem, o_act.n))

            def branch(q, body):
                def f(e):
                    most = e.value_load(MOSTI[0:1, 0:1], min_val=0, max_val=S)
                    with e.If(most > CAP):
                        body.run(e)
                q.do(f, tmost)

            branch(pe, o_pe)
            branch(dve, o_dve)
            branch(sca, o_act)
            xtok[0] = xtok[1] = dve.cp(SM[:, 121:122], SM[:, 120:121])

        def gate_rows(l, k, half):
            for h in range(2):
                B = 4 + h
                pe.wait(free[B], ada_tok[l])
                for c in range(4):
                    g = MODC[:, l, 8 * k + 4 * h + c:8 * k + 4 * h + c + 1].to_broadcast([P, P])
                    t = pe.mm(PS[:, B, c * P:c * P + P], g, ident, True, True, last=(c == 3))
                free[B] = t = sca.act(GB[:, h * 512:h * 512 + 512], PS[:, B, :], ACT.Copy, t, *xtok,
                                      scale=0.5 if half else 1.0)
            return t


        def norm_mod(l, k):
            g = VC[:, VAT["norm_g_2"][0], VAT["norm_g_2"][1] + (l * 3 + k) * 8:VAT["norm_g_2"][1] + (l * 3 + k) * 8 + 8]
            sc = SM[:, 8:16]
            t = dve.stt(sc, MODC[:, l, (3 * k + 1) * 8:(3 * k + 2) * 8], 1.0, g, ADD, MUL, ada_tok[l])
            return norm_turn(lambda c: sc[:, c:c + 1], lambda c: MODC[:, l, 3 * k * 8 + c:3 * k * 8 + c + 1], t)

        def ffn_second(l, i):
            xt = norm_mod(l, 2 * i)
            tg = gate_rows(l, 6 * i + 2, True)
            T = M2[:, 0:1024]

            def finish(b, y, t):
                k = dve.tt(T, y, GB[:, :], MUL, t, tg, *xtok)
                xtok[b] = dve.tt(X[:, b, :], X[:, b, :], T, ADD, k)
                return xtok[b]
            swiglu(xt, F2, A["ffn_wg_2"][l, i], A["ffn_wu_2"][l, i], A["ffn_wd_2"][l, i], finish)

        def mix_second(l):
            lam_init = 0.8 - 0.6 * float(np.exp(-0.3 * l))
            xt = norm_mod(l, 1)
            tgb = gate_rows(l, 5, True)
            tz = pool.ms(KZ[:, :], 0.0, *xtok)
            tp = project(A["w_in_2"][l], 2304, xt)
            lp = LP[:, l, :].rearrange("p (a d) -> p a d", d=64)
            lt, lv = SM[:, 16:144].rearrange("p (a d) -> p a d", d=64), SM[:, 144:146]
            t = dve.tt(lt, lp[:, 0::2, :], lp[:, 1::2, :], MUL, tsm)
            t = dve.red(lv, lt, ADD, t)
            t = sca.act(lv, lv, ACT.Exp, t)
            nlam = SM[:, 146:147]
            t = dve.tt(nlam, lv[:, 1:2], lv[:, 0:1], SUB, t)
            tlam = dve.ts(nlam, nlam, -lam_init, None, ADD, None, t)
            tq = [None, None]
            for lo, n, gi, so in ((0, 8, 0, 0), (512, 2, 1, 8)):
                x = heads(lo, n)
                sq = TMP[:, 0:2 * n * 64].rearrange("p (b h d) -> p b h d", b=2, d=64)
                ss = SM[:, 64:84].rearrange("p (b h) -> p b h", b=2)[:, :, so:so + n]
                t = norm_heads(x, n, P, 2, 64, sq, ss, QG2[:, l, gi, :], *tp, tsm, tlam, *tq)
                m = 2 * n
                ra = TMP[:, 1024:1024 + n * 64].rearrange("p (m s j) -> p m s j", s=2, j=32)
                rb = TMP[:, 1536:1536 + n * 64].rearrange("p (m s j) -> p m s j", s=2, j=32)
                for b in range(2):
                    cs = C[:, CA + 64 * b:CA + 64 * b + 64].rearrange("p (q s j) -> p q s j", q=2, j=16)
                    for s in range(2):
                        v = x[:, b, :, 32 * s:32 * s + 32].rearrange("p h (t j) -> p h t j", t=2)
                        a_ = ra[:, 0:n, s, :].rearrange("p h (t j) -> p h t j", t=2)
                        b_ = rb[:, 0:n, s, :].rearrange("p h (t j) -> p h t j", t=2)
                        sh = [P, n, 2, 16]
                        ta = dve.tt(a_, v, bc(cs[:, 0, s, :], sh, (1, 1)), MUL, t, tq[s])
                        tb = dve.tt(b_, v, bc(cs[:, 1, s, :], sh, (1, 1)), MUL, t, tq[s])
                        dve.tt(v[:, :, 0, :], a_[:, :, 0, :], b_[:, :, 1, :], SUB, ta, tb)
                        tq[b] = dve.tt(v[:, :, 1, :], a_[:, :, 1, :], b_[:, :, 0, :], ADD, ta, tb)
            tqa = tq[1]
            for k, lo in ((0, 0), (1, 768)):
                for b in range(2):
                    B = 4 + b
                    pe.wait(free[B], tqa, *tp)
                    for pr in range(4):
                        t = pe.tr(PS[:, B, pr * P:pr * P + P], PRB[:, b, lo + pr * P:lo + pr * P + P], ident,
                                  last=(pr == 3))
                    free[B] = tqt = sca.cp(QT[:, 4 * k:4 * k + 4, b * P:b * P + P],
                                           PS[:, B, :].rearrange("p (c n) -> p c n", c=4), t)
            KA = KZ[:, 0:1024].rearrange("p (v r n) -> p v r n", v=2, r=2)
            KD = KZ[:, 1024:3072].rearrange("p (c r n) -> p c r n", c=4, r=2)
            SW = TMP[:, 2048:2304].rearrange("p (b n) -> p b n", b=2)
            for b in range(2):
                dve.cp(SW[:, b, 0:64], PRB[:, b, 576:640], tqa)
                tsw = dve.cp(SW[:, b, 64:128], PRB[:, b, 512:576], tqa)
            pe.wait(free[6], tsw)
            for b in range(2):
                pe.tr(PS[:, 6, b * P:b * P + P], PRB[:, b, 512:640], ident)
                t = pe.tr(PS[:, 6, 256 + b * P:256 + b * P + P], SW[:, b, :], ident, last=(b == 1))
            dve.cp(KA[0:64, 0, 0, :], PS[0:64, 6, 0:256], t, tz)
            dve.cp(KA[64:128, 1, 1, :], PS[64:128, 6, 0:256], t)
            dve.cp(KA[0:64, 1, 0, :], PS[0:64, 6, 256:512], t)
            free[6] = tk = dve.cp(KA[64:128, 0, 1, :], PS[64:128, 6, 256:512], t)
            for hf in range(2):
                B = 7
                pe.wait(free[B])
                for b in range(2):
                    for c in range(2):
                        t = pe.tr(PS[:, B, c * 256 + b * P:c * 256 + b * P + P],
                                  PRB[:, b, 1280 + (2 * hf + c) * P:1280 + (2 * hf + c) * P + P], ident,
                                  last=(b == 1 and c == 1))
                for c in range(2):
                    dve.cp(KD[0:64, 2 * hf + c, 0, :], PS[0:64, B, c * 256:c * 256 + 256], t)
                    free[B] = tkd = dve.cp(KD[64:128, 2 * hf + c, 1, :], PS[64:128, B, c * 256:c * 256 + 256], t)

            bg = VAT["b_gate_2"]
            hb = SM[:, 448:464]
            thb = dve.ts(hb, VC[:, bg[0], bg[1] + 16 * l:bg[1] + 16 * l + 16], 0.5, None, MUL, None, tvc)
            gsl = {}
            tgs = [None]

            def gate_unit(u):
                ab, ch0 = u % 2, 2 * (u // 2)
                if u % 4 < 2:
                    q = u // 4
                    gsl[ab] = slab((A["w_gate_2"][l][:, ab * D + 512 * q:ab * D + 512 * q + 512]
                                    .rearrange("(c p) n -> p c n", p=P), 0, 8, 512))
                (w,), tw, slot = gsl[ab]
                pe.wait(free[7], tw)
                for k in range(2):
                    o = (ch0 + k) % 4 * P
                    for c in range(8):
                        t = pe.mm(PS[:, 7, k * 256:k * 256 + 256], w[:, c, o:o + P], XT[:, c, :], c == 0, c == 7,
                                  last=(c == 7 and k == 1))
                if u % 4 >= 2:
                    rel[slot] = t
                for k in range(2):
                    j = 8 * ab + ch0 + k
                    free[7] = tgs[0] = sca.act(GS[:, ch0 + k, ab * 256:ab * 256 + 256],
                                               PS[:, 7, k * 256:k * 256 + 256], ACT.Tanh, t, thb,
                                               scale=0.5, bias=hb[:, j:j + 1])

            at = Attn()
            oa = [None, None]
            od = [None, None]
            OD = M2[:, 1024:2048].rearrange("p (b n) -> p b n", b=2)
            coef = {}

            def grouped(b, v):
                so = 264 + 8 * (b * 2 + v)
                mx, sm = SM[:, so:so + 4], SM[:, so + 4:so + 8]

                def scores(s0):
                    pe.wait(tqt, tk)
                    for j in range(4):
                        t = pe.mm(PS[:, s0 + j // 2, (j % 2) * 256:(j % 2) * 256 + 256],
                                  QT[:, (4 * v + j) // 2, b * P:b * P + P], KA[:, v, j % 2, :], True, True, last=(j == 3))
                    return t

                def soft(s0, i, t, pf):
                    s4 = PS[:, s0:s0 + 2, :].rearrange("p k (j n) -> p (k j) n", j=2)
                    t = dve.red(mx, s4, MAX, t, neg=True)
                    t = dve.ts(mx, mx, 0.125, None, MUL, None, t)
                    for j in range(4):
                        te = sca.act(PB[:, i % 2, j * 256:j * 256 + 256], s4[:, j, :], ACT.Exp, t, pf,
                                     bias=mx[:, j:j + 1], scale=0.125, acc=sm[:, j:j + 1])
                    return te

                def values(i, te):
                    B = 6
                    pe.wait(*te, free[B])
                    for j in range(4):
                        h = 4 * v + j
                        for kc in range(2):
                            t = pe.mm(PS[:, B, h * 64:h * 64 + 64], PTB[:, i % 2, kc * 512 + j * P:kc * 512 + j * P + P],
                                      PRB[:, kc, 640 + v * 64:640 + v * 64 + 64], kc == 0, kc == 1,
                                      last=(j == 3 and kc == 1))
                    o4 = PS[:, B, v * 256:v * 256 + 256].rearrange("p (h d) -> p h d", d=64)
                    dst = OA[:, b, v * 256:v * 256 + 256].rearrange("p (h d) -> p h d", d=64)
                    k = dve.rcp(sm, sm, *te)
                    free[B] = oa[b] = dve.tt(dst, o4, bc(sm, [P, 4, 64], (2,)), MUL, t, k)
                    return t

                at.group(256, 4, scores, soft, None, values)

            def diff(b, hp):
                so = 320 + 8 * (b * 2 + hp)
                mx, sm = SM[:, so:so + 4], SM[:, so + 4:so + 8]

                def scores(s0):
                    pe.wait(tqt, tkd)
                    for j in range(4):
                        m, r = j // 2, j % 2
                        pr = 2 * m + hp
                        t = pe.mm(PS[:, s0 + m, r * 256:r * 256 + 256], QT[:, 4 + pr, b * P:b * P + P], KD[:, pr, r, :],
                                  True, True, last=(j == 3))
                    return t

                def soft(s0, i, t, pf):
                    s4 = PS[:, s0:s0 + 2, :].rearrange("p k (j n) -> p (k j) n", j=2)
                    for r in range(2):
                        slope = 2.0 ** (-2.0 * (2 * hp + r + 1))
                        v = s4[:, r::2, :]
                        dist = bc(C[:, CD + 256 * b:CD + 256 * b + 256], [P, 2, 256], (1,))
                        t = dve.stt(v, dist, -8.0 * slope, v, MUL, ADD, t)
                    t = dve.red(mx, s4, MAX, t, neg=True)
                    t = dve.ts(mx, mx, 0.125, None, MUL, None, t)
                    e4 = PB[:, i % 2, :].rearrange("p (j n) -> p j n", j=4)
                    for j in range(4):
                        te = sca.act(e4[:, j, :], s4[:, j, :], ACT.Exp, t, pf, bias=mx[:, j:j + 1], scale=0.125,
                                     acc=sm[:, j:j + 1])
                    return te

                def post(i, te):
                    e4 = PB[:, i % 2, :].rearrange("p (j n) -> p j n", j=4)
                    k = dve.rcp(sm, sm, te)
                    k = dve.ts(sm[:, 2:4], sm[:, 2:4], nlam, None, MUL, None, k, tlam)
                    for r in range(2):
                        k1 = dve.ts(e4[:, 2 + r, :], e4[:, 2 + r, :], sm[:, 2 + r:3 + r], None, MUL, None, k)
                        te = dve.stt(e4[:, r, :], e4[:, r, :], sm[:, r:r + 1], e4[:, 2 + r, :], MUL, ADD, k1)
                    return te

                def values(i, te):
                    B = 6
                    pe.wait(*te, free[B])
                    for r in range(2):
                        h = 2 * hp + r
                        for kc in range(2):
                            t = pe.mm(PS[:, B, h * P:h * P + P], PTB[:, i % 2, kc * 512 + r * P:kc * 512 + r * P + P],
                                      PRB[:, kc, 1792 + h * P:1792 + h * P + P], kc == 0, kc == 1,
                                      last=(r == 1 and kc == 1))
                    free[B] = od[b] = dve.cp(OD[:, b, hp * 256:hp * 256 + 256], PS[:, B, hp * 256:hp * 256 + 256], t)
                    return t

                at.group(256, 2, scores, soft, post, values)

            for b in range(2):
                for hp in range(2):
                    diff(b, hp)
                    gate_unit(2 * b + hp)
            for b in range(2):
                for v in range(2):
                    grouped(b, v)
                    gate_unit(4 + 2 * b + v)
            at.flush()
            x = OD.rearrange("p b (h d) -> p b h d", d=P)
            sq = TMP[:, 0:1024].rearrange("p (b h d) -> p b h d", b=2, d=P)
            ss = SM[:, 64:72].rearrange("p (b h) -> p b h", b=2)
            dve.wait(*at.tfree)
            t = norm_heads(x, 4, P, 2, P, sq, ss, SG[:, l, :], *od)
            tod = dve.ts(OD, OD, 1.0 - lam_init, None, MUL, None, t)
            for k, src in ((0, OA), (1, OD)):
                for b in range(2):
                    B = 2 * k + b
                    pe.wait(free[B], oa[b], tod)
                    for c in range(4):
                        t = pe.tr(PS[:, B, c * P:c * P + P], src[:, b, c * P:c * P + P], ident, last=(c == 3))
                    free[B] = tmt = sca.cp(MT[:, 4 * k:4 * k + 4, b * P:b * P + P],
                                           PS[:, B, :].rearrange("p (c n) -> p c n", c=4), t)
            MX = QT
            tm = None
            for q in range(2):
                f = q * 512
                (wab, wbb), tw, slot = slab(
                    (A["w_ba_2"][l][:, f:f + 512].rearrange("(c p) n -> p c n", p=P), 0, 4, 512),
                    (A["w_bb_2"][l][:, f:f + 512].rearrange("(c p) n -> p c n", p=P), 2048, 4, 512))
                for cc in range(4):
                    ch = 4 * q + cc
                    B = 4 + cc
                    o = cc * P
                    pe.wait(free[B], tw, tmt)
                    for k, w in ((0, wab), (1, wbb)):
                        for c in range(4):
                            t = pe.mm(PS[:, B, k * 256:k * 256 + 256], w[:, c, o:o + P], MT[:, 4 * k + c, :], c == 0,
                                      c == 3, last=(c == 3 and k == 1))
                    e = GS[:, ch, :]
                    free[B] = k = dve.stt(e, e, 1.0, PS[:, B, :], ADD, MUL, t, tgs[0])
                    tm = dve.tt(MX[:, ch, :], e[:, 0:256], e[:, 256:512], ADD, k)
                rel[slot] = t
            wo = [slab((A["w_o_2"][l][:, h * 512:h * 512 + 512].rearrange("(c p) n -> p c n", p=P), 0, 8, 512))
                  for h in range(2)]
            for b in range(2):
                for h, ((wt,), tw, slot) in enumerate(wo):
                    B = 2 * h + b
                    pe.wait(free[B], tw, tm)
                    for c in range(8):
                        t = pe.mm(PS[:, B, :], MX[:, c, b * P:b * P + P], wt[:, c, :], c == 0, c == 7, last=(c == 7))
                    xh = X[:, b, h * 512:h * 512 + 512]
                    T = M2[:, 0:512]
                    free[B] = k = dve.tt(T, PS[:, B, :], GB[:, h * 512:h * 512 + 512], MUL, t, tgb, *xtok)
                    xtok[b] = dve.tt(xh, xh, T, ADD, k)
                    rel[slot] = t

        mix_first(0)
        ffn_first()
        mix_first(1)
        moe()
        for l in range(2):
            ffn_second(l, 0)
            mix_second(l)
            ffn_second(l, 1)
        s_f, s_out = sem("s_f"), sem("s_out")
        sp.do(lambda e: e.dma_start(GB[:, :], A["final_g_2"].partition_broadcast(P)).then_inc(s_f, 16), *xtok)
        for b in range(2):
            t = sca.act(XS[b], X[:, b, :], ACT.Square, *xtok, acc=SM[:, b:b + 1])
            t = dve.ts(SM[:, 2 + b:3 + b], SM[:, b:b + 1], 1.0 / D, EPS, MUL, ADD, t)
            t = dve.rsqrt(SM[:, 4 + b:5 + b], SM[:, 2 + b:3 + b], SM[:, 6 + b:7 + b], t)
            t = dve.stt(XS[b], X[:, b, :], SM[:, 4 + b:5 + b], GB[:, :], MUL, MUL, t, (s_f, 16))
            o = out[0].rearrange("(b p) n -> b p n", p=P)[b]
            sp.do(lambda e, o=o, b=b: e.dma_start(o, XS[b]).then_inc(s_out, 16), t)
        sp.wait((s_out, 32))

        block = ctx.enter_context(nc.Block())

        @block.sync
        def _(e):
            sp.run(e)

        @block.gpsimd
        def _(e):
            pool.run(e)

        @block.scalar
        def _(e):
            sca.run(e)

        @block.vector
        def _(e):
            dve.run(e)

        @block.tensor
        def _(e):
            pe.run(e)


_INS = ['x', 'positions', 'attn_norm_g', 'ffn_norm_g', 'w_in', 'w_out', 'q_norm_g', 'k_norm_g', 'cmp_pos_k',
        'cmp_w1_k', 'cmp_w2_k', 'cmp_pos_v', 'cmp_w1_v', 'cmp_w2_v', 'conv_w', 'conv_b', 'conv_ln_g', 'conv_ln_b',
        'ffn_w_gate', 'ffn_w_up', 'ffn_w_down', 'moe_router', 'moe_w_gate', 'moe_w_up', 'moe_w_down', 'c_2',
        'ada_w_2', 'ada_b_2', 'norm_g_2', 'ffn_wg_2', 'ffn_wu_2', 'ffn_wd_2', 'w_in_2', 'qk_g_2', 'lam_p_2',
        'subln_g_2', 'w_ba_2', 'w_bb_2', 'w_gate_2', 'b_gate_2', 'w_o_2', 'final_g_2']


def kernel(**inputs):
    import numpy as _np
    import concourse.bacc as _bacc
    from concourse import mybir as _mybir
    from concourse.bass_utils import run_bass_kernel_spmd as _run

    nc = _bacc.Bacc("TRN2", target_bir_lowering=False, num_devices=1)
    arrays, args = {}, {}
    for name in _INS:
        a = _np.ascontiguousarray(inputs[name])
        arrays[f"in_{name}_dram"] = a
        args[name] = nc.dram_tensor(f"in_{name}_dram", a.shape, _mybir.dt.from_np(a.dtype), kind="ExternalInput").ap()
    c = constants()
    arrays["in_cst_dram"] = c
    args["cst"] = nc.dram_tensor("in_cst_dram", c.shape, _mybir.dt.float32, kind="ExternalInput").ap()
    o = nc.dram_tensor("out_0_dram", (1, S, D), _mybir.dt.float32, kind="ExternalOutput").ap()
    build(nc, args, o)
    r = _run(nc, [arrays], core_ids=[0])
    return r.results[0]["out_0_dram"]
```
